# Optimizing a Trainium2 kernel written in Bass

```python
import math
import jax, jax.numpy as jnp
from jax import lax
import numpy as np

D_MODEL = 1024
BATCH = 1
SEQ = 128
DEPTH = 2
DEC_BATCH = 1
DEC_SEQ = 1024
PAST_LEN = 128

GRID_W = 64
N_MIXERS = 3
N_SC = len(range(0, DEPTH, N_MIXERS))
N_MLA = len(range(1, DEPTH, N_MIXERS))
N_HY = len(range(2, DEPTH, N_MIXERS))
D_FF = 4 * D_MODEL
MOD_CHUNKS = 6
EPS = 1e-6
N_HEADS = 16
QK_NOPE = 64
ROPE_DIM = 32
AXIS_ROPE = ROPE_DIM // 2
QK_DIM = QK_NOPE + ROPE_DIM
V_DIM = 64
Q_RANK = 384
KV_RANK = 256
ROPE_THETA = 10000.0
Q_BLOCK = 128
HY_EMB = 33
HY_BANDS = (HY_EMB - 1) // 2
HY_ORDER = 64
HY_TARGET = 1e-2
HY_FAST = 0.3
HY_SLOW = 1.5

kernel_name = 'hybrid_conv_mla_hyena_diffusion_step'

F32 = jnp.float32

def rmsnorm(x, g):
    xf = x.astype(F32)
    y = xf * lax.rsqrt(jnp.mean(xf * xf, axis=-1, keepdims=True) + EPS)
    return (y * g.astype(F32)).astype(x.dtype)

def dwconv3(u, w, b):
    up = jnp.pad(u, ((0, 0), (1, 1), (0, 0)))
    return up[:, :-2] * w[0] + up[:, 1:-1] * w[1] + up[:, 2:] * w[2] + b

def short_conv_mixer(h, w_in, conv_w, conv_b, w_out):
    bg, cg, xv = jnp.split(h @ w_in, 3, axis=-1)
    u = dwconv3(cg * xv, conv_w, conv_b)
    return (bg * u) @ w_out

def hyena_filter(n, w0, b0, w1, b1, w2, b2, w3, freq):
    t01 = jnp.linspace(0.0, 1.0, n, dtype=F32)[:, None]
    w = 2.0 * math.pi * jnp.arange(n, dtype=F32)[:, None] / n
    fb = jnp.linspace(1e-4, HY_BANDS - 1, HY_BANDS, dtype=F32)[None, :]
    z = jnp.concatenate([t01, jnp.cos(fb * w), -jnp.sin(fb * w)], axis=-1)
    fr = freq.astype(F32)
    a = jnp.sin(fr * (z @ w0.astype(F32) + b0.astype(F32)))
    a = jnp.sin(fr * (a @ w1.astype(F32) + b1.astype(F32)))
    a = jnp.sin(fr * (a @ w2.astype(F32) + b2.astype(F32)))
    hf, hb = jnp.split(a @ w3.astype(F32), 2, axis=-1)
    deltas = jnp.abs(jnp.linspace(math.log(HY_TARGET) / HY_SLOW, math.log(HY_TARGET) / HY_FAST,
                                  D_MODEL, dtype=F32))
    decay = jnp.exp(-t01 * deltas)
    hf = hf * decay
    hb = hb * decay
    filt = jnp.concatenate([hf, jnp.zeros((1, D_MODEL), F32), hb[1:][::-1]], axis=0)
    return filt / jnp.sum(jnp.abs(filt), axis=0, keepdims=True)

def long_conv(v, filt):
    n = v.shape[1]
    vf = jnp.fft.rfft(v.astype(F32), n=2 * n, axis=1)
    ff = jnp.fft.rfft(filt, axis=0)
    y = jnp.fft.irfft(vf * ff[None], n=2 * n, axis=1)[:, :n]
    return y.astype(v.dtype)

def hyena_mixer(h, w_in, conv_w, conv_b, w0, b0, w1, b1, w2, b2, w3, freq, bias, w_out):
    n = h.shape[1]
    x0, x1, v = jnp.split(dwconv3(h @ w_in, conv_w, conv_b), 3, axis=-1)
    filt = hyena_filter(n, w0, b0, w1, b1, w2, b2, w3, freq)
    v = v * x1
    v = long_conv(v, filt) + v * bias
    return (v * x0) @ w_out

def grid_positions(n):
    rows = n // GRID_W
    row = jnp.repeat(jnp.arange(rows), GRID_W)
    col = jnp.tile(jnp.arange(GRID_W), rows)
    return row, col

def axial_rope(x, row, col):
    inv = jnp.power(ROPE_THETA, -jnp.arange(0, AXIS_ROPE, 2, dtype=F32) / AXIS_ROPE)

    def rot(xa, pos):
        ang = pos.astype(F32)[:, None] * inv[None]
        cos = jnp.cos(ang)[None, :, None, :].astype(xa.dtype)
        sin = jnp.sin(ang)[None, :, None, :].astype(xa.dtype)
        x1, x2 = jnp.split(xa, 2, axis=-1)
        return jnp.concatenate([x1 * cos - x2 * sin, x2 * cos + x1 * sin], axis=-1)

    xr, xc = jnp.split(x, 2, axis=-1)
    return jnp.concatenate([rot(xr, row), rot(xc, col)], axis=-1)

def rope_tail(x, row, col):
    return jnp.concatenate([x[..., :QK_NOPE], axial_rope(x[..., QK_NOPE:], row, col)], axis=-1)

def mla_queries(h, w_dq, q_norm_g, w_uq, qn_g):
    b, n, _ = h.shape
    q = (rmsnorm(h @ w_dq, q_norm_g) @ w_uq).reshape(b, n, N_HEADS, QK_DIM)
    return rmsnorm(q, qn_g)

def mla_latent_kv(h, w_dkv, kv_norm_g):
    ckv, kpe = jnp.split(h @ w_dkv, [KV_RANK], axis=-1)
    return rmsnorm(ckv, kv_norm_g), kpe

def mla_expand(ckv, kpe, w_ukv, kn_g):
    b, n, _ = ckv.shape
    kn, v = jnp.split((ckv @ w_ukv).reshape(b, n, N_HEADS, QK_NOPE + V_DIM), [QK_NOPE], axis=-1)
    k = jnp.concatenate([kn, jnp.broadcast_to(kpe[:, :, None, :], (b, n, N_HEADS, ROPE_DIM))], axis=-1)
    return rmsnorm(k, kn_g), v

def block_attention(q, k, v):
    b, n, h, dk = q.shape
    nb = n // Q_BLOCK
    qb = jnp.moveaxis(q.reshape(b, nb, Q_BLOCK, h, dk), 1, 0)
    scale = dk ** -0.5

    def one(qblk):
        s = jnp.einsum('bqhd,bkhd->bhqk', qblk, k, preferred_element_type=F32) * scale
        p = jax.nn.softmax(s, axis=-1).astype(v.dtype)
        return jnp.einsum('bhqk,bkhd->bqhd', p, v)

    o = lax.map(one, qb)
    return jnp.moveaxis(o, 0, 1).reshape(b, n, h * v.shape[-1])

def mla_context(h, P, j):
    q = mla_queries(h, P['mla_w_dq'][j], P['mla_q_norm_g'][j], P['mla_w_uq'][j], P['mla_qn_g'][j])
    ckv, kpe = mla_latent_kv(h, P['mla_w_dkv'][j], P['mla_kv_norm_g'][j])
    k, v = mla_expand(ckv, kpe, P['mla_w_ukv'][j], P['mla_kn_g'][j])
    return block_attention(q, k, v) @ P['mla_w_o'][j], ckv, kpe

def mla_latent(h, ctx_ckv, ctx_kpe, P, j):
    row, col = grid_positions(h.shape[1])
    q = rope_tail(mla_queries(h, P['mla_w_dq'][j], P['mla_q_norm_g'][j], P['mla_w_uq'][j],
                              P['mla_qn_g'][j]), row, col)
    ckv, kpe = mla_latent_kv(h, P['mla_w_dkv'][j], P['mla_kv_norm_g'][j])
    k, v = mla_expand(ckv, kpe, P['mla_w_ukv'][j], P['mla_kn_g'][j])
    k = rope_tail(k, row, col)
    kc, vc = mla_expand(ctx_ckv, ctx_kpe, P['mla_w_ukv'][j], P['mla_kn_g'][j])
    o = block_attention(q, jnp.concatenate([k, kc], axis=1), jnp.concatenate([v, vc], axis=1))
    return o @ P['mla_w_o'][j]

def trunk(x, cond, P, cache_ckv=None, cache_kpe=None):
    is_context = cache_ckv is None
    ckvs, kpes = [], []
    for i in range(DEPTH):
        kind, j = i % N_MIXERS, i // N_MIXERS
        sh1, sc1, g1, sh2, sc2, g2 = jnp.split(jax.nn.silu(cond) @ P['mod_w'][i] + P['mod_b'][i],
                                               MOD_CHUNKS, axis=-1)
        h = rmsnorm(x, P['norm1_g'][i]) * (1 + sc1) + sh1
        if kind == 0:
            y = short_conv_mixer(h, P['sc_w_in'][j], P['sc_conv_w'][j], P['sc_conv_b'][j], P['sc_w_out'][j])
        elif kind == 1:
            if is_context:
                y, ckv, kpe = mla_context(h, P, j)
                ckvs.append(ckv)
                kpes.append(kpe)
            else:
                y = mla_latent(h, cache_ckv[:, j], cache_kpe[:, j], P, j)
        else:
            y = hyena_mixer(h, P['hy_w_in'][j], P['hy_conv_w'][j], P['hy_conv_b'][j],
                            P['hy_f_w0'][j], P['hy_f_b0'][j], P['hy_f_w1'][j], P['hy_f_b1'][j],
                            P['hy_f_w2'][j], P['hy_f_b2'][j], P['hy_f_w3'][j], P['hy_sin_freq'][j],
                            P['hy_bias'][j], P['hy_w_out'][j])
        x = x + g1 * y
        h = rmsnorm(x, P['norm2_g'][i]) * (1 + sc2) + sh2
        x = x + g2 * (jnp.square(jax.nn.relu(h @ P['mlp_w1'][i])) @ P['mlp_w2'][i])
    return x, ckvs, kpes

def setup_inputs(seed: int = 0) -> dict:
    key = jax.random.key(seed)
    ks = iter(jax.random.split(key, 64))

    def nrm(shape, scale):
        return scale * jax.random.normal(next(ks), shape, F32)

    def gain(shape):
        return 1.0 + nrm(shape, 0.02)

    D = D_MODEL
    return {
        'x_prompt': nrm((BATCH, SEQ, D), 1.0),
        'x_sample': nrm((DEC_BATCH, DEC_SEQ, D), 1.0),
        'cache_ckv': nrm((DEC_BATCH, N_MLA, PAST_LEN, KV_RANK), 1.0),
        'cache_kpe': nrm((DEC_BATCH, N_MLA, PAST_LEN, ROPE_DIM), 1.0),
        'c': nrm((DEC_BATCH, D), 1.0),
        'c_ctx': nrm((D,), 1.0),
        'norm1_g': gain((DEPTH, D)),
        'norm2_g': gain((DEPTH, D)),
        'mod_w': nrm((DEPTH, D, MOD_CHUNKS * D), 0.5 * D ** -0.5),
        'mod_b': nrm((DEPTH, MOD_CHUNKS * D), 0.02),
        'mlp_w1': nrm((DEPTH, D, D_FF), D ** -0.5),
        'mlp_w2': nrm((DEPTH, D_FF, D), D_FF ** -0.5),
        'sc_w_in': nrm((N_SC, D, 3 * D), D ** -0.5),
        'sc_conv_w': nrm((N_SC, 3, D), 3 ** -0.5),
        'sc_conv_b': nrm((N_SC, D), 0.02),
        'sc_w_out': nrm((N_SC, D, D), D ** -0.5),
        'mla_w_dq': nrm((N_MLA, D, Q_RANK), D ** -0.5),
        'mla_q_norm_g': gain((N_MLA, Q_RANK)),
        'mla_w_uq': nrm((N_MLA, Q_RANK, N_HEADS * QK_DIM), Q_RANK ** -0.5),
        'mla_w_dkv': nrm((N_MLA, D, KV_RANK + ROPE_DIM), D ** -0.5),
        'mla_kv_norm_g': gain((N_MLA, KV_RANK)),
        'mla_w_ukv': nrm((N_MLA, KV_RANK, N_HEADS * (QK_NOPE + V_DIM)), KV_RANK ** -0.5),
        'mla_qn_g': gain((N_MLA, QK_DIM)),
        'mla_kn_g': gain((N_MLA, QK_DIM)),
        'mla_w_o': nrm((N_MLA, N_HEADS * V_DIM, D), (N_HEADS * V_DIM) ** -0.5),
        'hy_w_in': nrm((N_HY, D, 3 * D), D ** -0.5),
        'hy_conv_w': nrm((N_HY, 3, 3 * D), 3 ** -0.5),
        'hy_conv_b': nrm((N_HY, 3 * D), 0.02),
        'hy_f_w0': nrm((N_HY, HY_EMB, HY_ORDER), HY_EMB ** -0.5),
        'hy_f_b0': nrm((N_HY, HY_ORDER), 0.02),
        'hy_f_w1': nrm((N_HY, HY_ORDER, HY_ORDER), HY_ORDER ** -0.5),
        'hy_f_b1': nrm((N_HY, HY_ORDER), 0.02),
        'hy_f_w2': nrm((N_HY, HY_ORDER, HY_ORDER), HY_ORDER ** -0.5),
        'hy_f_b2': nrm((N_HY, HY_ORDER), 0.02),
        'hy_f_w3': nrm((N_HY, HY_ORDER, 2 * D), HY_ORDER ** -0.5),
        'hy_sin_freq': gain((N_HY, HY_ORDER)),
        'hy_bias': nrm((N_HY, D), 0.1),
        'hy_w_out': nrm((N_HY, D, D), D ** -0.5),
    }

def reference(x_prompt, x_sample, cache_ckv, cache_kpe, c, c_ctx, norm1_g, norm2_g, mod_w, mod_b,
              mlp_w1, mlp_w2, sc_w_in, sc_conv_w, sc_conv_b, sc_w_out, mla_w_dq, mla_q_norm_g,
              mla_w_uq, mla_w_dkv, mla_kv_norm_g, mla_w_ukv, mla_qn_g, mla_kn_g, mla_w_o, hy_w_in,
              hy_conv_w, hy_conv_b, hy_f_w0, hy_f_b0, hy_f_w1, hy_f_b1, hy_f_w2, hy_f_b2, hy_f_w3,
              hy_sin_freq, hy_bias, hy_w_out):
    P = dict(norm1_g=norm1_g, norm2_g=norm2_g, mod_w=mod_w, mod_b=mod_b, mlp_w1=mlp_w1,
             mlp_w2=mlp_w2, sc_w_in=sc_w_in, sc_conv_w=sc_conv_w, sc_conv_b=sc_conv_b,
             sc_w_out=sc_w_out, mla_w_dq=mla_w_dq, mla_q_norm_g=mla_q_norm_g, mla_w_uq=mla_w_uq,
             mla_w_dkv=mla_w_dkv, mla_kv_norm_g=mla_kv_norm_g, mla_w_ukv=mla_w_ukv,
             mla_qn_g=mla_qn_g, mla_kn_g=mla_kn_g, mla_w_o=mla_w_o, hy_w_in=hy_w_in,
             hy_conv_w=hy_conv_w, hy_conv_b=hy_conv_b, hy_f_w0=hy_f_w0, hy_f_b0=hy_f_b0,
             hy_f_w1=hy_f_w1, hy_f_b1=hy_f_b1, hy_f_w2=hy_f_w2, hy_f_b2=hy_f_b2, hy_f_w3=hy_f_w3,
             hy_sin_freq=hy_sin_freq, hy_bias=hy_bias, hy_w_out=hy_w_out)
    y_prompt, ckvs, kpes = trunk(x_prompt, c_ctx[None, None, :], P)
    new_ckv = jnp.stack(ckvs, axis=1)
    new_kpe = jnp.stack(kpes, axis=1)
    y_sample, _, _ = trunk(x_sample, c[:, None, :], P, cache_ckv, cache_kpe)
    return (y_prompt, y_sample, new_ckv, new_kpe)


_drawn_inputs = setup_inputs


def setup_inputs(seed=0):
    import zlib

    import numpy as np

    out = dict(_drawn_inputs(seed))
    spreads = {}
    factors = {'cache_ckv': 8.0,
     'cache_kpe': 8.0,
     'norm2_g': 4.735,
     'sc_conv_b': 8.0,
     'mla_q_norm_g': 8.0,
     'mla_kv_norm_g': 8.454,
     'mla_qn_g': 8.0,
     'mla_kn_g': 8.0}
    for name, (base, spread) in spreads.items():
        noise = np.random.default_rng([zlib.crc32(name.encode()), seed]).standard_normal(out[name].shape)
        drawn = base * np.exp(spread * noise) if base else spread * noise
        out[name] = __import__('jax').numpy.asarray(drawn.astype(out[name].dtype))
    for name, factor in factors.items():
        out[name] = (out[name] * factor).astype(out[name].dtype)
    return out
```

```python
from contextlib import ExitStack

import concourse.bass as bass
from concourse import mybir
from concourse.alu_op_type import AluOpType as ALU

ACT = mybir.ActivationFunctionType
AX_X = mybir.AxisListType.X
F32 = mybir.dt.float32
F32R = mybir.dt.float32r
ds = bass.ds

P = 128
D = 1024
KT = D // P
NS, NP = 1024, 128
N = NS + NP
NT = N // P
TB = 384
BANK = 512
FF = 4 * D
HT = 4
CHUNKS = FF // (HT * P)
MODS = 6 * KT
FIRST_MODS = 2 * KT
MOD_SLOTS = 8
EPS = 1e-6
HEADS, NOPE, ROPE, QK, VD = 16, 64, 32, 96, 64
QR, KVR = 384, 256
QT, CT = QR // P, KVR // P
KEYS = N + 128
KTILES = KEYS // P
PROMPT_K, CACHE_K = 8, 9
PAIRS = HEADS // 2
AUG = NT
QROWS = QK + AUG
SCALE = float(QK) ** -0.5
WSLOT = 1024
LAYERS = 2
STEPS = 19
STEP = [(k, q * 512, 512, q) for q in range(2) for k in (0, 1, 2, 3, 4, 5, 6, 7, CACHE_K)] + [(PROMPT_K, NS, NP, 2)]
PR = 3
SPLIT_AT = 4
TURN_AT = 5
TURNS = 2 + 2 * NT + (1 + 3 + 1 if LAYERS > 1 else 0) + 2 * NT

BLOCKS_IN, BLOCKS_OUT, BLOCKS_CHUNK = 3 * KT, KT, 2 * HT
MLP_BLOCKS = CHUNKS * BLOCKS_CHUNK
B_IN = 0
B_OUT = B_IN + BLOCKS_IN
B_MLP0 = B_OUT + BLOCKS_OUT
B_LAT = B_MLP0 + MLP_BLOCKS
B_ATT = B_LAT + QT + CT + 1
B_WO = B_ATT + 2 * PAIRS
B_MLP1 = B_WO + BLOCKS_OUT
B_END = B_MLP1 + MLP_BLOCKS

VEC = {}
_row = 0
for _name, _rows in (("norm1_g", 2 * KT), ("norm2_g", 2 * KT), ("conv_w", 3 * KT), ("conv_b", KT),
                     ("c", KT), ("c_ctx", KT), ("q_norm_g", QT), ("kv_norm_g", CT)):
    VEC[_name] = (_row, _row + _rows)
    _row += _rows
VROWS = _row


def block_dmas(b):
    if B_ATT <= b <= B_WO:
        return 3 if (b - B_ATT) % 2 == 0 else 2
    return 1


def block_words(b):
    if B_ATT <= b < B_WO:
        return QT * 2 * QK + CT * 2 * NOPE if (b - B_ATT) % 2 == 0 else CT * 2 * VD
    return WSLOT


def raw_loaded(b):
    return 16 * sum(block_dmas(k) for k in range(b % 2, b + 1, 2))


def block_stages(b):
    if B_ATT <= b < B_WO:
        return 0
    for start in (B_MLP0, B_MLP1):
        if start <= b < start + MLP_BLOCKS:
            return 1 if (b - start) % BLOCKS_CHUNK < HT else 2
    return 1


NORM_STAGES = {B_IN: 1, B_MLP0: 1, B_LAT: 1, B_ATT: 2, B_MLP1: 1}


def stages_through(b):
    return sum(block_stages(k) for k in range(0, b + 1)) + sum(n for k, n in NORM_STAGES.items() if k <= b + 1)


U_V, U_TURN, U_QK, U_MAX = 3, 6, 8, 1
U_PAIR = U_V + U_TURN + U_QK + U_MAX + U_TURN + U_MAX
U_LEAD = U_QK + U_TURN + U_MAX


def attention_released(b):
    p, odd = divmod(b - B_ATT, 2)
    if odd:
        return U_LEAD + p * U_PAIR + U_V
    return U_QK if p == 0 else U_LEAD + (p - 1) * U_PAIR + U_V + U_TURN + U_QK


class Place:

    def __init__(self, **at):
        self.at, self.step, self.i = dict(at), {}, None

    def enter(self, i, **step):
        self.i, self.step, self.entered = i, step, dict(self.at)

    def leave(self, turns):
        for k, n in self.step.items():
            assert self.at[k] - self.entered[k] == n, (k, self.at[k] - self.entered[k], n)
            self.at[k] = self.entered[k] + n * turns
        for k in self.at:
            assert k in self.step or self.at[k] == self.entered[k], k
        self.i, self.step = None, {}

    def count(self, key, back=0, f=lambda n: n):
        n = self.at[key] - back
        v = f(n)
        if self.i is None or not self.step.get(key):
            return v
        return self.i * (f(n + self.step[key]) - v) + v


def build(nc, T, outs):
    y_prompt, y_sample, new_ckv, new_kpe = outs
    with ExitStack() as ctx:
        def sem(name):
            return ctx.enter_context(nc.semaphore(name))

        cursor = [(nc.sbuf_base + 31) // 32 * 32]

        def at(name, shape, dt, offset):
            return nc.alloc_sbuf_tensor_at(name, shape, dt, offset=offset)

        def new(name, shape, dt=F32):
            words = 1
            for n in shape[1:]:
                words *= n
            t = at(name, shape, dt, cursor[0])
            cursor[0] += (words * 4 + 31) // 32 * 32
            return t

        ident = new("ident", [P, P])
        ones = new("ones", [P, P])
        trig = new("trig", [P, 2, NT, ROPE])
        eps = new("eps", [P, 1])
        vec = new("vec", [P, VROWS])
        mod_bias = new("mod_bias", [P, 2 * MODS])
        mod = new("mod", [P, 2 * MODS, 2])
        cond = new("cond", [P, KT, 2])
        cond_tmp = new("cond_tmp", [P, KT, 2])
        gain = new("gain", [P, 4, KT, 2])
        rstd = new("rstd", [P, N])
        rot_cos, rot_sin, rot_a, rot_b = (
            at(f"rot{k}", [P, NT, ROPE], F32, cursor[0] - N * 4 + k * NT * ROPE * 4) for k in range(4))
        kpe = new("kpe", [P, KTILES, ROPE])
        kpe_rot = new("kpe_rot", [P, KTILES, ROPE])
        kpe_sq = new("kpe_sq", [P, KTILES])
        g_q = new("g_q", [P, QK])
        g_k = new("g_k", [P, QK])
        g_qk = new("g_qk", [P, NOPE])

        w_raw = [new(f"w_raw{s}", [P, WSLOT]) for s in range(2)]
        w_hi = [new(f"w_hi{s}", [P, WSLOT], F32R) for s in range(2)]
        w_lo = [new(f"w_lo{s}", [P, WSLOT], F32R) for s in range(2)]

        G0 = cursor[0]
        v32 = new("v32", [P, KT, N])
        hid_hi = at("hid_hi", [P, HT, N], F32R, G0)
        hid_lo = at("hid_lo", [P, HT, N], F32R, G0 + HT * N * 4)
        mod_first = at("mod_first", [P, MOD_SLOTS, WSLOT], F32, G0)
        ql = at("ql", [P, QT, N], F32, G0)
        ckv = at("ckv", [P, CT, KEYS], F32, G0 + QT * N * 4)
        kpe_t = at("kpe_t", [P, N], F32, G0 + QT * N * 4 + CT * KEYS * 4)
        cache_in = at("cache_in", [P, KVR], F32, G0 + (QT + 1) * N * 4 + CT * KEYS * 4)
        ckv_out = at("ckv_out", [P, KVR], F32, G0 + (QT + 1) * N * 4 + CT * KEYS * 4 + KVR * 4)
        o32 = at("o32", [P, KT, N], F32, G0)

        H0 = cursor[0]
        h_hi = new("h_hi", [P, KT, N], F32R)
        h_lo = new("h_lo", [P, KT, N], F32R)
        x_in = at("x_in", [P, NT, D], F32, H0)
        vec_in = at("vec_in", [P, 2, P], F32, H0 + NT * D * 4)
        y_out = at("y_out", [P, NT, D], F32, H0)
        ql_hi = at("ql_hi", [P, QT, N], F32R, H0)
        ql_lo = at("ql_lo", [P, QT, N], F32R, H0 + QT * N * 4)
        ckv_hi = at("ckv_hi", [P, CT, KEYS], F32R, H0 + 2 * QT * N * 4)
        ckv_lo = at("ckv_lo", [P, CT, KEYS], F32R, H0 + 2 * QT * N * 4 + CT * KEYS * 4)
        A0 = H0 + 2 * QT * N * 4 + 2 * CT * KEYS * 4

        x = new("x", [P, KT, N])
        mod_raw = [new(f"mod_raw{s}", [P, WSLOT]) for s in range(2)]
        TW = N + 4
        tmp = [new(f"tmp{s}", [P, TW]) for s in range(4)]
        TOP = cursor[0]
        assert TOP <= nc.sbuf_usable_end, (TOP, nc.sbuf_usable_end)

        cursor[0] = A0
        q_tok = new("q_tok", [P, NT, 2, QK])
        k_tok = new("k_tok", [P, KTILES, 2, QK])
        v_hi = new("v_hi", [P, KTILES, 3 * VD], F32R)
        v_lo = new("v_lo", [P, KTILES, 3 * VD], F32R)
        qT_hi = [new(f"qT_hi{s}", [QROWS, N], F32R) for s in range(2)]
        qT_lo = [new(f"qT_lo{s}", [QROWS, N], F32R) for s in range(2)]
        kT_hi = [new(f"kT_hi{s}", [QROWS, KEYS], F32R) for s in range(2)]
        kT_lo = [new(f"kT_lo{s}", [QROWS, KEYS], F32R) for s in range(2)]
        p32, p_lo, p_hi = [], [], []
        for s in range(PR):
            p32.append(new(f"p32_{s}", [P, BANK]))
            p_lo.append(at(f"p_lo{s}", [P, BANK], F32R, cursor[0] - BANK * 4))
            p_hi.append(new(f"p_hi{s}", [P, BANK], F32R))
        inv = [new(f"inv{s}", [P, BANK]) for s in range(2)]
        junk = new("junk", [P, 4, QK])
        ssq = new("ssq", [P, 2 * NT + 2 * KTILES])
        r_tok = new("r_tok", [P, 2 * NT + 2 * KTILES])
        row_max = new("row_max", [P, NT])
        assert cursor[0] <= TOP, (cursor[0], TOP)

        ps = nc.alloc_psum_tensor("ps", [P, 8 * BANK], F32)

        def bank(k, n=BANK):
            return ps[:, k * BANK:k * BANK + n]

        def stage_ps(s):
            return ps[:, 3 * (s % 2) * BANK:3 * (s % 2 + 1) * BANK].rearrange("p (t n) -> p t n", t=3)[:, :, 0:TB]

        def parts(s, tile):
            v = stage_ps(s)
            return [(v[:, 0:2, :], tile[:, 0:2 * TB].rearrange("p (t n) -> p t n", t=2), 0),
                    (v[:, 2, 0:NS - 2 * TB], tile[:, 2 * TB:NS], 0),
                    (v[:, 2, NS - 2 * TB:TB], tile[:, NS:N], 1)]

        def cols3(tile):
            return tile.rearrange("p (t n) -> p t n", t=3)

        def unit_ps(k):
            return (7, 0, 1, 2)[k % 4] * BANK

        SEGS = ((0, NS, 0), (NS, N, 1))

        w_loaded = [sem(f"w_loaded{s}") for s in range(2)]
        m_loaded = [sem(f"m_loaded{s}") for s in range(2)]
        mf_loaded = [sem(f"mf_loaded{s}") for s in range(MOD_SLOTS)]
        x_loaded = [sem(f"x_loaded{s}") for s in range(3)]
        w_hi_done = sem("w_hi_done")
        w_lo_done = sem("w_lo_done")
        mod_mm = sem("mod_mm")
        mod_done = sem("mod_done")
        stage_done = sem("stage_done")
        stage_free = sem("stage_free")
        const_in = sem("const_in")
        gains_in = sem("gains_in")
        vec_loaded = sem("vec_loaded")
        turn_mm = sem("turn_mm")
        turn_out = sem("turn_out")
        cond_act = sem("cond_act")
        cond_ready = sem("cond_ready")
        gain_done = sem("gain_done")
        sq_done = sem("sq_done")
        acc_done = sem("acc_done")
        rstd_done = sem("rstd_done")
        dve_self = sem("dve_self")
        t_done = sem("t_done")
        h_hi_done = sem("h_hi_done")
        h_lo_done = sem("h_lo_done")
        relu_done = sem("relu_done")
        hid_hi_done = sem("hid_hi_done")
        hid_lo_done = sem("hid_lo_done")
        y_stored = sem("y_stored")
        x_spilled = sem("x_spilled")
        x_back = sem("x_back")
        cache_loaded = sem("cache_loaded")
        new_stored = sem("new_stored")
        arena_ready = sem("arena_ready")
        unit_done = sem("unit_done")
        unit_hi = sem("unit_hi")
        unit_free = sem("unit_free")
        max_mm = sem("max_mm")
        max_free = sem("max_free")
        ssq_done = sem("ssq_done")
        r_log = sem("r_log")
        r_done = sem("r_done")
        tok_ready = sem("tok_ready")
        s_mm = sem("s_mm")
        p_exp = sem("p_exp")
        p_hi_done = sem("p_hi_done")
        p_lo_done = sem("p_lo_done")
        p_free = sem("p_free")
        inv_log = sem("inv_log")
        inv_done = sem("inv_done")
        o_free = sem("o_free")
        pads_ready = sem("pads_ready")
        x_dram = nc.dram_tensor("x_spill", [P, KT, N], F32, kind="Internal").ap()

        def rows(ap):
            return ap.rearrange("(k p) n -> p k n", p=P)

        mod_v = [rows(T["mod_w"][l]) for l in range(2)]
        w1_v = [rows(T["mlp_w1"][l]) for l in range(2)]
        w2_v = [rows(T["mlp_w2"][l]) for l in range(2)]
        win_v, wout_v = rows(T["sc_w_in"][0]), rows(T["sc_w_out"][0])
        dq_v, dkv_v = rows(T["mla_w_dq"][0]), rows(T["mla_w_dkv"][0])
        uq_v, ukv_v = rows(T["mla_w_uq"][0]), rows(T["mla_w_ukv"][0])
        wo_v = rows(T["mla_w_o"][0])

        block = ctx.enter_context(nc.Block())

        @block.sync
        def _(sp):
            L = Place(b=0, m=FIRST_MODS)

            def load(*pieces):
                s = L.at["b"] % 2
                for piece in pieces:
                    sp.lower_ap_dma(piece[3])
                if L.i is not None or L.at["b"] >= 2:
                    sp.wait_ge(w_lo_done, L.count("b", 1))
                for off, kt, n, src in pieces:
                    dst = w_raw[s][:, off:off + kt * n].rearrange("p (k n) -> p k n", k=kt)
                    sp.dma_start(dst, src).then_inc(w_loaded[s], 16)
                L.at["b"] += 1

            def load_mod(l, col):
                s = L.at["m"] % 2
                src = mod_v[l][:, :, ds(col, P)]
                sp.lower_ap_dma(src)
                if L.i is not None or L.at["m"] >= FIRST_MODS + 2:
                    sp.wait_ge(mod_mm, L.count("m", 1))
                sp.dma_start(mod_raw[s][:, :].rearrange("p (k n) -> p k n", k=KT), src).then_inc(m_loaded[s], 16)
                L.at["m"] += 1

            sp.dma_start(vec_in[0:2 * MODS, 0, :], T["mod_b"].rearrange("l (m p) -> (l m) p", p=P)).then_inc(vec_loaded, 16)
            for name, src in (("norm1_g", T["norm1_g"].rearrange("l (m p) -> (l m) p", p=P)),
                              ("norm2_g", T["norm2_g"].rearrange("l (m p) -> (l m) p", p=P)),
                              ("conv_w", T["sc_conv_w"].rearrange("l w (m p) -> (l w m) p", p=P)),
                              ("conv_b", T["sc_conv_b"].rearrange("l (m p) -> (l m) p", p=P)),
                              ("c", T["c"].rearrange("l (m p) -> (l m) p", p=P)),
                              ("c_ctx", T["c_ctx"].rearrange("(m p) -> m p", p=P)),
                              ("q_norm_g", T["mla_q_norm_g"].rearrange("l (m p) -> (l m) p", p=P)),
                              ("kv_norm_g", T["mla_kv_norm_g"].rearrange("l (m p) -> (l m) p", p=P))):
                a, z = VEC[name]
                sp.dma_start(vec_in[a:z, 1, :], src).then_inc(vec_loaded, 16)
            sp.dma_start(ident[:, :], T["ident"]).then_inc(const_in, 16)
            xs = T["x_sample"][0].rearrange("(t p) n -> p t n", p=P)
            for g in range(2):
                sp.dma_start(x_in[:, 4 * g:4 * g + 4, :], xs[:, 4 * g:4 * g + 4, :]).then_inc(x_loaded[g], 16)
            sp.dma_start(x_in[:, NS // P, :], T["x_prompt"][0]).then_inc(x_loaded[2], 16)
            for m in range(FIRST_MODS):
                if m >= MOD_SLOTS:
                    sp.wait_ge(mod_mm, m - MOD_SLOTS + 1)
                sp.dma_start(mod_first[:, m % MOD_SLOTS, :].rearrange("p (k n) -> p k n", k=KT),
                             mod_v[0][:, :, m * P:(m + 1) * P]).then_inc(mf_loaded[m % MOD_SLOTS], 16)
            sp.dma_start(trig[:, :, :, :], T["trig"]).then_inc(gains_in, 16)
            sp.dma_start(kpe[:, CACHE_K, :], T["cache_kpe"][0, 0]).then_inc(gains_in, 16)
            sp.dma_start(g_q[:, :], T["mla_qn_g"].to_broadcast([P, QK])).then_inc(gains_in, 16)
            sp.dma_start(g_k[:, :], T["mla_kn_g"].to_broadcast([P, QK])).then_inc(gains_in, 16)

            def load_in(f, m):
                for k, part in enumerate((1, 2, 0)):
                    load((0, KT, P, win_v[:, :, ds(f * P + part * D, P)]))
                    load_mod(0, m * P + k * P)

            load_in(0, FIRST_MODS)
            load_in(1, FIRST_MODS + 3)
            with sp.Fori(1, KT // 2) as i:
                L.enter(i - 1, b=6, m=6)
                for f in range(2):
                    load_in(i * 2 + f, i * 6 + (FIRST_MODS + 3 * f))
                L.leave(KT // 2 - 1)
            with sp.Fori(0, KT // 2) as i:
                L.enter(i, b=2, m=2)
                for j in range(2):
                    load((0, KT, P, wout_v[:, :, ds(i * 2 * P + j * P, P)]))
                    load_mod(0, i * 2 * P + (5 * KT + j) * P)
                L.leave(KT // 2)

            def load_mlp(l, mods):
                with sp.Fori(0, CHUNKS) as c:
                    L.enter(c, b=2 * HT, m=6 if mods else 0)
                    for k in range(2 * HT):
                        if k < HT:
                            load((0, KT, P, w1_v[l][:, :, ds(c * HT * P + k * P, P)]))
                        else:
                            load((0, HT, 2 * P, w2_v[l][:, ds(c * HT, HT), (k - HT) * 2 * P:(k - HT + 1) * 2 * P]))
                        if mods and k < 6:
                            load_mod(1, c * 6 * P + k * P)
                    L.leave(CHUNKS)

            load_mlp(0, True)
            if LAYERS > 1:
                for col in (0, P):
                    load((0, KT, P, dq_v[:, :, col:col + P]))
                sp.wait_ge(stage_done, stages_through(B_LAT - 1))
                sp.dma_start(cache_in[:, :], T["cache_ckv"][0, 0]).then_inc(cache_loaded, 16)
                load((0, KT, P, dq_v[:, :, 2 * P:3 * P]))
                for col in (0, P, KVR + ROPE - P):
                    load((0, KT, P, dkv_v[:, :, col:col + P]))
                with sp.Fori(0, PAIRS) as p:
                    L.enter(p, b=2)
                    load((0, QT, 2 * QK, uq_v[:, :, ds(p * 2 * QK, 2 * QK)]),
                         *[(QT * 2 * QK + h * CT * NOPE, CT, NOPE, ukv_v[:, :, ds(p * 256 + h * 128, NOPE)])
                           for h in range(2)])
                    load(*[(h * CT * VD, CT, VD, ukv_v[:, :, ds(p * 256 + (h * 128 + NOPE), VD)]) for h in range(2)])
                    L.leave(PAIRS)
                load(*[(a * P, z - a, P, wo_v[:, a:z, 0:P]) for a, z in ((0, 3), (3, 6), (6, KT))])
                load((0, KT, P, wo_v[:, :, P:2 * P]))
                sp.wait_ge(o_free, 2 + 3 * HEADS)
                sp.dma_start(x[:, :, :], x_dram).then_inc(x_back, 16)
                with sp.Fori(1, KT // 2) as i:
                    L.enter(i - 1, b=2)
                    for j in range(2):
                        load((0, KT, P, wo_v[:, :, ds(i * 2 * P + j * P, P)]))
                    L.leave(KT // 2 - 1)
                load_mlp(1, False)
            for t in range(NT):
                sp.wait_ge(turn_out, TURNS - 2 * NT + 2 * t + 2)
                dst = y_prompt[0] if t == NT - 1 else y_sample[0, t * P:(t + 1) * P, :]
                sp.dma_start(dst, y_out[:, t, :]).then_inc(y_stored, 16)
            sp.wait_ge(y_stored, 16 * NT)

        @block.gpsimd
        def _(pool):
            L = Place(b=0)
            A = Place(j=0)
            pool.memset(ones[:, :], 1.0).then_inc(stage_free, 1)
            pool.memset(eps[:, :], EPS).then_inc(stage_free, 1)

            def split_lo(words=WSLOT):
                s = L.at["b"] % 2
                pool.wait_ge(w_hi_done, L.count("b", -1))
                pool.tensor_tensor(w_lo[s][:, 0:words], w_raw[s][:, 0:words], w_hi[s][:, 0:words].bitcast(F32),
                                   ALU.subtract).then_inc(w_lo_done, 1)
                L.at["b"] += 1

            def split_pairs(n):
                with pool.Fori(0, n) as i:
                    L.enter(i, b=2)
                    split_lo()
                    split_lo()
                    L.leave(n)

            def p_low(head, j):
                n = NP if j == STEPS - 1 else BANK
                s = (head * STEPS + j) % PR
                pool.wait_ge(p_hi_done, A.count("j", -1))
                pool.tensor_tensor(p_lo[s][:, 0:n], p32[s][:, 0:n], p_hi[s][:, 0:n].bitcast(F32),
                                   ALU.subtract).then_inc(p_lo_done, 1)
                A.at["j"] += 1

            split_pairs((B_ATT if LAYERS > 1 else B_LAT) // 2)
            if LAYERS > 1:
                pool.wait_ge(h_lo_done, 4 * KT + QT + CT)
                pool.wait_ge(x_spilled, 16)
                done = {}
                for part, value, signal in ((v_hi[:, :, VD:2 * VD], 1.0, p_free), (v_lo[:, :, VD:2 * VD], 0.0, p_free),
                                            (qT_lo[0][QK:QROWS, :], 0.0, p_free),
                                            (kT_lo[0][QK:QROWS, :], 0.0, o_free), (kT_lo[1][QK:QROWS, :], 0.0, o_free),
                                            (kT_hi[0][QK:QROWS, :], 1.0, arena_ready),
                                            (kT_hi[1][QK:QROWS, :], 1.0, arena_ready),
                                            (qT_lo[1][QK:QROWS, :], 0.0, arena_ready)):
                    pool.memset(part.bitcast(F32), value).then_inc(signal, 1)
                    done[signal.name] = done.get(signal.name, 0) + 1
                    pool.wait_ge(signal, done[signal.name])
                split_lo(block_words(B_ATT))
                split_lo(block_words(B_ATT + 1))
                split_lo(block_words(B_ATT))
                with pool.Fori(0, PAIRS - 1) as p:
                    L.enter(p, b=2)
                    A.enter(p, j=2 * STEPS)
                    for head in range(2):
                        for j in range(STEPS):
                            p_low(head, j)
                            if j == SPLIT_AT:
                                split_lo(block_words(B_ATT + 1) if head == 0 else WSLOT)
                    A.leave(PAIRS - 1)
                    L.leave(PAIRS - 1)
                for head in range(2):
                    for j in range(STEPS):
                        p_low(head, j)
                split_lo()
                split_pairs((B_END - B_WO - 2) // 2)

        @block.scalar
        def _(act):
            L = Place(b=0, s=2, hid=0)
            C = dict(sq=0, acc=0, t=0, h=0)
            A = Place(j=0, u=0, g=0, r=0)

            def split_hi(words=WSLOT):
                b = L.at["b"]
                s = b % 2
                act.wait_ge(w_loaded[s], L.count("b", 0, raw_loaded))
                if B_ATT <= b - 2 < B_WO:
                    act.wait_ge(unit_done, L.count("b", 2, attention_released))
                elif L.i is not None or b >= 2:
                    act.wait_ge(stage_done, L.count("b", 2, stages_through))
                act.activation(w_hi[s][:, 0:words], w_raw[s][:, 0:words], ACT.Copy).then_inc(w_hi_done, 1)
                L.at["b"] += 1

            def rms(src, n, width):
                for j in range(n):
                    before = C["acc"] + (max(j - 2, 1) if j >= 2 else 0)
                    if before:
                        act.wait_ge(acc_done, before)
                    act.activation(tmp[j % 2][:, 0:N], src(j), ACT.Square).then_inc(sq_done, 1)
                C["acc"] += n - 1
                act.wait_ge(stage_done, L.at["s"] - 1)
                act.activation(cols3(rstd[:, :]), stage_ps(L.at["s"]), ACT.Ln, bias=eps[:, 0:1],
                               scale=1.0 / width).then_inc(stage_free, 1)
                L.at["s"] += 1
                act.wait_ge(stage_free, L.at["s"])
                act.activation(rstd[:, :], rstd[:, :], ACT.Exp, scale=-0.5).then_inc(rstd_done, 1)

            def norm(layer, which):
                act.wait_ge(stage_free, L.at["s"])
                rms(lambda j: x[:, j, :], KT, D)
                shift = layer * MODS + 3 * which * KT
                for j in range(KT):
                    act.wait_ge(t_done, C["t"] + 1)
                    for a, z, c in SEGS:
                        ins = act.activation(h_hi[:, j, a:z], tmp[j % 2][:, a:z], ACT.Identity,
                                             bias=mod[:, shift + j, c:c + 1])
                    ins.then_inc(h_hi_done, 1)
                    C["t"] += 1

            def split_rows(src):
                for j in range(KT):
                    act.activation(h_hi[:, j, :], src[:, j, :], ACT.Copy).then_inc(h_hi_done, 1)

            def out_blocks(apart=False):
                def two():
                    for j in range(2):
                        split_hi()
                        L.at["s"] += 1
                if apart:
                    two()
                n = KT // 2 - apart
                with act.Fori(0, n) as i:
                    L.enter(i, b=2, s=2)
                    two()
                    L.leave(n)

            def chunk(last=False):
                for k in range(2 * HT):
                    if not (last and k == 2 * HT - 1):
                        split_hi()
                    if k < HT:
                        act.wait_ge(stage_done, L.count("s", 1))
                        act.activation(cols3(tmp[0][:, 0:N]), stage_ps(L.at["s"]), ACT.Relu).then_inc(relu_done, 1)
                        L.at["s"] += 1
                        act.wait_ge(stage_free, L.count("s"))
                        act.activation(hid_hi[:, k, :], tmp[1][:, 0:N], ACT.Copy).then_inc(hid_hi_done, 1)
                        L.at["hid"] += 1
                    else:
                        L.at["s"] += 2

            def mlp(last=False):
                n = CHUNKS - 1 if last else CHUNKS
                with act.Fori(0, n) as c:
                    L.enter(c, b=2 * HT, s=3 * HT, hid=HT)
                    chunk()
                    L.leave(n)
                if last:
                    chunk(True)

            act.wait_ge(turn_out, 2)
            for k, name in enumerate(("c", "c_ctx")):
                a, z = VEC[name]
                ins = act.activation(cond_tmp[:, :, k], vec[:, a:z], ACT.Exp, scale=-1.0)
            ins.then_inc(cond_act, 1)
            act.wait_ge(turn_out, 2 + 2 * NT)
            split_hi()
            norm(0, 0)

            def in_blocks():
                for k in range(6):
                    split_hi()
                    if k % 3 == 0:
                        act.wait_ge(stage_done, L.count("s", 1))
                        act.wait_ge(stage_free, L.count("s"))
                        act.activation(cols3(tmp[0][:, 0:N]), stage_ps(L.at["s"]), ACT.Copy).then_inc(stage_free, 1)
                    L.at["s"] += 1

            with act.Fori(0, KT // 2) as i:
                L.enter(i, b=6, s=6)
                in_blocks()
                L.leave(KT // 2)
            act.wait_ge(stage_free, L.at["s"])
            split_rows(v32)
            out_blocks()
            norm(0, 1)
            mlp(last=LAYERS == 1)
            if LAYERS > 1:
                norm(1, 0)
                for k in range(QT + CT + 1):
                    split_hi(block_words(L.at["b"]))
                    L.at["s"] += 1
                    if k == 0:
                        act.wait_ge(h_lo_done, 4 * KT)
                        act.dma_start(x_dram, x[:, :, :]).then_inc(x_spilled, 16)
                act.wait_ge(stage_free, L.at["s"])
                rms(lambda j: ql[:, j, :], QT, QR)
                for j in range(QT):
                    act.wait_ge(t_done, C["t"] + 1)
                    act.activation(ql_hi[:, j, :], ql[:, j, :], ACT.Copy).then_inc(h_hi_done, 1)
                    C["t"] += 1
                rms(lambda j: ckv[:, j, 0:N], CT, KVR)
                for j in range(CT):
                    act.wait_ge(t_done, C["t"] + 1)
                    act.activation(ckv_hi[:, j, :], ckv[:, j, :], ACT.Copy).then_inc(h_hi_done, 1)
                    C["t"] += 1
                act.wait_ge(turn_out, TURNS - 2 * NT)
                act.dma_start(new_ckv[0, 0], ckv_out[:, :]).then_inc(new_stored, 16)
                act.dma_start(new_kpe[0, 0], kpe[:, PROMPT_K, :]).then_inc(new_stored, 16)

                def unit_high(out, in_):
                    act.wait_ge(unit_done, A.count("u", -1))
                    act.activation(out, in_, ACT.Copy).then_inc(unit_hi, 1)
                    A.at["u"] += 1

                def v_units(k):
                    for a, z in groups(KTILES, 4):
                        b0 = unit_ps(k)
                        unit_high(v_cols(v_hi, a, z), ps[:, b0:b0 + (z - a) * 2 * VD].rearrange(
                            "p (t h n) -> p t h n", h=2, n=VD))
                        k += 1

                def turn_units(k, s):
                    for dst, tiles in ((qT_hi[s], NT), (kT_hi[s], KTILES)):
                        for a, z in groups(tiles, 4):
                            b0 = unit_ps(k)
                            unit_high(dst[0:QK, a * P:z * P], ps[0:QK, b0:b0 + (z - a) * P])
                            k += 1

                def token_rstd():
                    act.wait_ge(ssq_done, A.count("r", -1))
                    act.activation(r_tok[:, :], ssq[:, :], ACT.Ln, bias=eps[:, 0:1], scale=1.0 / QK).then_inc(r_log, 1)
                    act.wait_ge(r_log, A.count("r", -1))
                    act.activation(r_tok[:, :], r_tok[:, :], ACT.Exp, scale=-0.5).then_inc(r_done, 1)
                    A.at["r"] += 1

                def step(head, j):
                    n = NP if j == STEPS - 1 else BANK
                    pos = head * STEPS + j
                    s = pos % PR
                    act.wait_ge(s_mm, A.count("j", -1))
                    act.wait_ge(p_free, A.count("j", -2 if pos < 2 else -1))
                    act.activation(p32[s][:, 0:n], bank(3 + pos % 2, n), ACT.Exp, scale=SCALE).then_inc(p_exp, 1)
                    act.wait_ge(p_exp, A.count("j", -1))
                    act.activation(p_hi[s][:, 0:n], p32[s][:, 0:n], ACT.Copy).then_inc(p_hi_done, 1)
                    A.at["j"] += 1

                def inverse(head, qb, behind):
                    n = NP if qb == 2 else BANK
                    g = head * 3 + qb
                    to, of = (slice(0, VD), slice(VD, P)) if head == 0 else (slice(VD, P), slice(0, VD))
                    act.wait_ge(p_free, A.count("j", behind - PR))
                    act.wait_ge(o_free, A.count("g", -1))
                    pv = ps[of, (5 + g % 2) * BANK:(5 + g % 2) * BANK + n]
                    act.activation(inv[g % 2][to, 0:n], pv, ACT.Ln).then_inc(inv_log, 1)
                    act.wait_ge(inv_log, A.count("g", -1))
                    act.activation(inv[g % 2][to, 0:n], inv[g % 2][to, 0:n], ACT.Exp, scale=-1.0).then_inc(inv_done, 1)
                    A.at["g"] += 1

                def pair(last):
                    for head in range(2):
                        for j in range(STEPS):
                            step(head, j)
                            if head == 0 and j == 1:
                                v_units(0)
                                turn_units(U_V, 1)
                                if not last:
                                    A.at["u"] += U_QK
                            if head == 0 and j == STEPS - 1:
                                A.at["u"] += U_MAX
                            if head == 1 and j == TURN_AT + 2 and not last:
                                turn_units(U_V + U_TURN + U_QK + U_MAX, 0)
                                A.at["u"] += U_MAX
                            if j == SPLIT_AT and not last:
                                split_hi(block_words(B_ATT + 1) if head == 0 else WSLOT)
                            if j == 12:
                                inverse(head, 0, 4)
                            if head == 0 and j == 15 and not last:
                                token_rstd()
                        inverse(head, 1, 1)
                        inverse(head, 2, 0)

                split_hi(block_words(B_ATT + 1))
                A.at["u"] += U_QK
                token_rstd()
                turn_units(U_QK, 0)
                split_hi(block_words(B_ATT))
                A.at["u"] += U_MAX
                with act.Fori(0, PAIRS - 1) as p:
                    L.enter(p, b=2)
                    A.enter(p, j=2 * STEPS, u=U_PAIR, g=6, r=1)
                    pair(False)
                    A.leave(PAIRS - 1)
                    L.leave(PAIRS - 1)
                pair(True)
                act.wait_ge(o_free, 2 + 3 * HEADS)
                split_rows(o32)
                out_blocks(apart=True)
                norm(1, 1)
                mlp(last=True)

        @block.tensor
        def _(pe):
            L = Place(b=0, s=2, m=0, hid=0)
            C = dict(turn=0, acc=0, h=0)

            def three(outs, k, first, last, lhs, rhs):
                ins = None
                for n, (a, b) in enumerate(((0, 0), (0, 1), (1, 0))):
                    for out, cols in outs:
                        ins = pe.matmul(out, lhs[a], rhs[b](cols), start=first and n == 0, stop=last and n == 2)
                return ins

            def stage(w0, tiles, src, ready=None):
                s, slot = L.at["s"], L.at["b"] % 2
                pe.wait_ge(stage_free, L.count("s", 1))
                v = stage_ps(s)
                for k in range(tiles):
                    if ready:
                        ready(k)
                    w = w0(k)
                    ins = three([(v[:, t, :], t) for t in range(3)], k, k == 0, k == tiles - 1,
                                [w_hi[slot][:, w:w + P], w_lo[slot][:, w:w + P]],
                                [lambda t, r=r: r[:, k, t * TB:(t + 1) * TB] for r in src])
                ins.then_inc(stage_done, 1)
                L.at["s"] += 1

            def weights():
                pe.wait_ge(w_lo_done, L.count("b", -1))

            def h_block(ready=None):
                weights()
                stage(lambda k: k * P, KT, (h_hi, h_lo), ready)
                L.at["b"] += 1

            def h_ready(base):
                return lambda k: pe.wait_ge(h_lo_done, base + k + 1)

            def mod_tile(raw, loaded, count):
                b = 6 + L.at["m"] % 2
                pe.wait_ge(loaded, count)
                if L.i is not None or L.at["m"] >= 2:
                    pe.wait_ge(mod_done, L.count("m", 1))
                for k in range(KT):
                    ins = pe.matmul(bank(b, 2), raw[:, k * P:(k + 1) * P], cond[:, k, :], start=k == 0, stop=k == KT - 1)
                ins.then_inc(mod_mm, 1)
                L.at["m"] += 1

            def mod_next():
                m = L.at["m"]
                mod_tile(mod_raw[m % 2], m_loaded[m % 2],
                         L.count("m", 0, lambda n: 16 * ((n - FIRST_MODS) // 2 + 1)))

            def turn(pieces, out_free):
                b = 6 + C["turn"] % 2
                if out_free > 0:
                    pe.wait_ge(turn_out, out_free)
                for k, (src, rows_) in enumerate(pieces):
                    ins = pe.transpose(ps[:, b * BANK + k * P:b * BANK + k * P + rows_], src, ident[0:rows_, 0:rows_])
                ins.then_inc(turn_mm, 1)
                C["turn"] += 1

            def sum_squares(n):
                s = L.at["s"]
                C["acc"] += n - 1
                pe.wait_ge(acc_done, C["acc"])
                pe.wait_ge(stage_free, s - 1)
                for t in range(3):
                    ins = pe.matmul(stage_ps(s)[:, t, :], ones[:, :], tmp[2][:, t * TB:(t + 1) * TB], start=True, stop=True)
                ins.then_inc(stage_done, 1)
                L.at["s"] += 1

            def mlp(mods):
                hb = C["h"]
                with pe.Fori(0, CHUNKS) as c:
                    L.enter(c, b=2 * HT, s=3 * HT, m=6 if mods else 0, hid=HT)
                    for k in range(2 * HT):
                        if k < HT:
                            h_block(h_ready(hb) if k == 0 else None)
                        else:
                            weights()
                            for half in range(2):
                                def hid_ready(t):
                                    pe.wait_ge(hid_lo_done, L.count("hid", -t - 1))
                                stage(lambda t: t * 2 * P + half * P, HT, (hid_hi, hid_lo),
                                      hid_ready if k == HT and half == 0 else None)
                            L.at["b"] += 1
                        if mods and k < 6:
                            mod_next()
                    L.at["hid"] += HT
                    L.leave(CHUNKS)

            pe.wait_ge(vec_loaded, 16 * 9)
            pe.wait_ge(const_in, 16)
            turn([(vec_in[0:2 * MODS, 0, :], 2 * MODS)], 0)
            turn([(vec_in[0:VROWS, 1, :], VROWS)], 0)
            for t in range(NT):
                pe.wait_ge(x_loaded[t // 4], 16)
                for g in range(2):
                    turn([(x_in[:, t, (4 * g + k) * P:(4 * g + k + 1) * P], P) for k in range(4)], C["turn"] - 1)
            pe.wait_ge(cond_ready, 1)
            pe.wait_ge(turn_out, C["turn"])
            for m in range(FIRST_MODS):
                mod_tile(mod_first[:, m % MOD_SLOTS, :], mf_loaded[m % MOD_SLOTS], 16 * (m // MOD_SLOTS + 1))
            pe.wait_ge(stage_free, 2)
            sum_squares(KT)
            with pe.Fori(0, KT // 2) as i:
                L.enter(i, b=6, s=6, m=6)
                for k in range(6):
                    h_block(h_ready(0) if k == 0 else None)
                    mod_next()
                L.leave(KT // 2)
            C["h"] = KT

            def out_blocks(mods):
                with pe.Fori(0, KT // 2) as i:
                    L.enter(i, b=2, s=2, m=2 if mods else 0)
                    for k in range(2):
                        h_block(h_ready(C["h"]) if k == 0 else None)
                        if mods:
                            mod_next()
                    L.leave(KT // 2)
                C["h"] += KT

            out_blocks(True)
            sum_squares(KT)
            mlp(True)
            C["h"] += KT
            if LAYERS > 1:
                sum_squares(KT)
                for k in range(QT + CT + 1):
                    h_block(h_ready(C["h"]) if k == 0 else None)
                C["h"] += KT
                pe.wait_ge(mod_done, 2 * MODS)
                pe.wait_ge(cache_loaded, 16)
                turn([(cache_in[:, k * P:(k + 1) * P], P) for k in range(CT)], C["turn"] - 1)
                pe.wait_ge(stage_free, L.at["s"])
                for a, z in groups(NT, 4):
                    turn([(kpe_t[:, t * P:(t + 1) * P], P) for t in range(a, z)], C["turn"] - 1)
                sum_squares(QT)
                sum_squares(CT)
                pe.wait_ge(t_done, 3 * KT + QT + CT)
                turn([(ckv[:, k, NS:N], P) for k in range(CT)], C["turn"] - 1)

                A = Place(j=0, u=0, g=0, m=0, tok=0)
                C["h"] += QT + CT
                pe.wait_ge(h_lo_done, C["h"])
                pe.wait_ge(stage_free, L.at["s"])
                pe.wait_ge(arena_ready, 3)

                def unit(k, back=2):
                    if A.i is not None or A.at["u"] > back:
                        pe.wait_ge(unit_free, A.count("u", back))
                    return unit_ps(k)

                def unit_end(ins):
                    ins.then_inc(unit_done, 1)
                    A.at["u"] += 1

                def qk_units(k):
                    weights()
                    for a, z in groups(NT, 2):
                        b0 = unit(k)
                        for t in range(a, z):
                            out = ps[:, b0 + (t - a) * 2 * QK:b0 + (t - a + 1) * 2 * QK]
                            for kt in range(QT):
                                cols = slice(kt * 2 * QK, (kt + 1) * 2 * QK)
                                ins = three([(out, 0)], kt, kt == 0, kt == QT - 1,
                                            [r[:, kt, t * P:(t + 1) * P] for r in (ql_hi, ql_lo)],
                                            [lambda _, w=w: w[:, cols] for w in (w_hi[0], w_lo[0])])
                        unit_end(ins)
                        k += 1
                    kv_units(k, 0, QT * 2 * QK)

                def kv_units(k, slot, w0):
                    for a, z in groups(KTILES, 4):
                        b0 = unit(k)
                        for t in range(a, z):
                            out = ps[:, b0 + (t - a) * 2 * VD:b0 + (t - a + 1) * 2 * VD].rearrange(
                                "p (h n) -> p h n", h=2)
                            for kt in range(CT):
                                ins = three([(out, 0)], kt, kt == 0, kt == CT - 1,
                                            [r[:, kt, t * P:(t + 1) * P] for r in (ckv_hi, ckv_lo)],
                                            [lambda _, w=w: w[:, w0:w0 + 2 * CT * VD].rearrange(
                                                "p (h k n) -> p h k n", h=2, k=CT)[:, :, kt, :]
                                             for w in (w_hi[slot], w_lo[slot])])
                        unit_end(ins)
                        k += 1
                    L.at["b"] += 1

                def turn_units(k, head):
                    pe.wait_ge(tok_ready, A.count("tok"))
                    for src, tiles in ((q_tok, NT), (k_tok, KTILES)):
                        for a, z in groups(tiles, 4):
                            b0 = unit(k)
                            for t in range(a, z):
                                ins = pe.transpose(ps[0:QK, b0 + (t - a) * P:b0 + (t - a + 1) * P],
                                                   src[:, t, head, :], ident[:, :])
                            unit_end(ins)
                            k += 1

                def max_tile(s, t):
                    if t == 0:
                        pe.wait_ge(unit_free, A.count("u"))
                    if A.i is not None or A.at["m"] > 0:
                        pe.wait_ge(max_free, A.count("m"))
                    keys = [(PROMPT_K * P, P, 0)] if t == NT - 1 else [
                        (0, BANK, 0), (BANK, BANK, BANK), (CACHE_K * P, P, 2 * BANK)]
                    for c0, n, b0 in keys:
                        ins = pe.matmul(ps[:, b0:b0 + n], qT_hi[s][0:QK, t * P:(t + 1) * P],
                                        kT_hi[s][0:QK, c0:c0 + n], start=True, stop=True)
                    ins.then_inc(max_mm, 1)
                    A.at["m"] += 1

                def max_unit(k):
                    pe.wait_ge(max_free, A.count("m"))
                    b0 = unit(k)
                    unit_end(pe.transpose(ps[0:NT, b0:b0 + P], row_max[:, :], ident[:, :]))

                def scores(head, j):
                    pos = head * STEPS + j
                    kt, q0, n, _ = STEP[j]
                    if j == 0:
                        pe.wait_ge(unit_free, A.count("u"))
                    if j >= 2:
                        pe.wait_ge(p_exp, A.count("j", 1 - 2))
                    ins = three([(bank(3 + pos % 2, n), 0)], 0, True, True,
                                [r[head][:, kt * P:(kt + 1) * P] for r in (kT_hi, kT_lo)],
                                [lambda _, r=r: r[head][:, q0:q0 + n] for r in (qT_hi, qT_lo)])
                    ins.then_inc(s_mm, 1)

                def values(head, j):
                    pos = head * STEPS + j
                    kt, q0, n, qb = STEP[j]
                    g = head * 3 + qb
                    first, last = j in (0, 9, 18), j in (8, 17, 18)
                    if first:
                        pe.wait_ge(o_free, A.count("g", -1))
                    pe.wait_ge(p_lo_done, A.count("j", -1))
                    ins = three([(bank(5 + g % 2, n), 0)], 0, first, last,
                                [r[:, kt, head * VD:head * VD + P] for r in (v_hi, v_lo)],
                                [lambda _, r=r: r[pos % PR][:, 0:n] for r in (p_hi, p_lo)])
                    ins.then_inc(p_free, 1)
                    A.at["j"] += 1
                    if last:
                        A.at["g"] += 1

                def pair(last):
                    for head in range(2):
                        scores(head, 0)
                        A.at["j"] += 0
                        scores(head, 1)
                        if head == 0:
                            weights()
                            kv_units(0, 1, 0)
                            turn_units(U_V, 1)
                            if not last:
                                qk_units(U_V + U_TURN)
                                A.at["tok"] += 1
                            pe.wait_ge(unit_free, A.count("u", (0 if last else U_QK) + U_TURN))
                        for j in range(STEPS):
                            if j + 2 < STEPS:
                                scores(head, j + 2)
                            values(head, j)
                            if head == 0:
                                if 2 <= j < 2 + NT:
                                    max_tile(1, j - 2)
                                if j == 13:
                                    max_unit(U_V + U_TURN + U_QK)
                            elif not last:
                                k = U_V + U_TURN + U_QK + U_MAX
                                if j == TURN_AT:
                                    turn_units(k, 0)
                                if TURN_AT + 3 <= j < TURN_AT + 3 + NT:
                                    max_tile(0, j - TURN_AT - 3)
                                if j == STEPS - 1:
                                    max_unit(k + U_TURN)

                qk_units(0)
                A.at["tok"] += 1
                turn_units(U_QK, 0)
                for t in range(NT):
                    max_tile(0, t)
                max_unit(U_QK + U_TURN)
                with pe.Fori(0, PAIRS - 1) as p:
                    L.enter(p, b=2)
                    A.enter(p, j=2 * STEPS, u=U_PAIR, g=6, m=2 * NT, tok=1)
                    pair(False)
                    A.leave(PAIRS - 1)
                    L.leave(PAIRS - 1)
                pair(True)
                out_blocks(False)
                sum_squares(KT)
                mlp(False)
            pe.wait_ge(stage_free, L.at["s"])
            for t in range(NT):
                for g in range(2):
                    turn([(x[:, 4 * g + k, t * P:(t + 1) * P], P) for k in range(4)], C["turn"] - 1)
            assert C["turn"] == TURNS, C["turn"]

        @block.vector
        def _(dve):
            L = Place(b=0, s=2, m=0, hid=0)
            S = Place(n=0)
            C = dict(turn=0, sq=0, t=0, h=0, rstd=0)

            def own(ins):
                ins.then_inc(dve_self, 1)
                S.at["n"] += 1
                dve.wait_ge(dve_self, S.count("n"))

            def mod_out(index):
                dve.wait_ge(mod_mm, L.count("m", -1))
                b = 6 + L.at["m"] % 2
                dve.tensor_scalar(mod[:, ds(index, 1), :].rearrange("p a c -> p (a c)"), bank(b, 2),
                                  mod_bias[:, ds(index, 1)], None, ALU.add).then_inc(mod_done, 1)
                L.at["m"] += 1

            def turn_out_(outs):
                b = 6 + C["turn"] % 2
                dve.wait_ge(turn_mm, C["turn"] + 1)
                ins = outs(b * BANK)
                ins.then_inc(turn_out, 1)
                C["turn"] += 1

            def add_squares(n):
                for j in range(1, n):
                    dve.wait_ge(sq_done, C["sq"] + j + 1)
                    a = tmp[0] if j == 1 else tmp[2]
                    dve.tensor_tensor(tmp[2][:, 0:N], a[:, 0:N], tmp[j % 2][:, 0:N], ALU.add).then_inc(acc_done, 1)
                    C["acc"] = C.get("acc", 0) + 1
                    dve.wait_ge(acc_done, C["acc"])
                C["sq"] += n

            def norm(layer, which):
                n = 2 * layer + which
                scale = layer * MODS + (3 * which + 1) * KT
                dve.wait_ge(mod_done, scale + KT)
                g0 = VEC["norm1_g" if which == 0 else "norm2_g"][0] + layer * KT
                gv = vec[:, g0:g0 + KT].unsqueeze(2).to_broadcast([P, KT, 2])
                own(dve.scalar_tensor_tensor(gain[:, n, :, :], mod[:, scale:scale + KT, :], 1.0, gv,
                                             ALU.add, ALU.mult))
                add_squares(KT)
                C["rstd"] += 1
                dve.wait_ge(rstd_done, C["rstd"])
                L.at["s"] += 1
                shift = layer * MODS + 3 * which * KT

                def scaled(j):
                    dve.wait_ge(h_lo_done, C["h"]) if C["h"] else None
                    for a, z, c in SEGS:
                        ins = dve.scalar_tensor_tensor(tmp[j % 2][:, a:z], x[:, j, a:z], gain[:, n, j, c:c + 1],
                                                       rstd[:, a:z], ALU.mult, ALU.mult)
                    ins.then_inc(t_done, 1)
                    C["t"] += 1
                scaled(0)
                for j in range(KT):
                    if j + 1 < KT:
                        scaled(j + 1)
                    C["h"] += 1
                    dve.wait_ge(t_done, C["t"] - (1 if j + 1 < KT else 0))
                    dve.wait_ge(h_hi_done, C["h"])
                    for a, z, c in SEGS:
                        ins = dve.scalar_tensor_tensor(h_lo[:, j, a:z], tmp[j % 2][:, a:z],
                                                       mod[:, shift + j, c:c + 1], h_hi[:, j, a:z].bitcast(F32),
                                                       ALU.add, ALU.subtract)
                    ins.then_inc(h_lo_done, 1)

            def low_rows(dst, src, hi, n):
                for j in range(n):
                    C["h"] += 1
                    dve.wait_ge(h_hi_done, C["h"])
                    dve.tensor_tensor(dst[:, j, :], src[:, j, :], hi[:, j, :].bitcast(F32),
                                      ALU.subtract).then_inc(h_lo_done, 1)

            def residual(j, gate):
                dve.wait_ge(stage_done, L.count("s", 1))
                dve.wait_ge(stage_free, L.count("s"))
                tile = x[:, ds(j, 1), :].rearrange("p a n -> p (a n)")
                for v, xt, c in parts(L.at["s"], tile):
                    ins = dve.scalar_tensor_tensor(xt, v, mod[:, ds(gate, 1), c:c + 1].rearrange("p a c -> p (a c)"), xt,
                                                   ALU.mult, ALU.add)
                ins.then_inc(stage_free, 1)
                L.at["s"] += 1

            def out_blocks(layer, mods):
                with dve.Fori(0, KT // 2) as i:
                    L.enter(i, s=2, m=2 if mods else 0)
                    for k in range(2):
                        residual(i * 2 + k, i * 2 + (layer * MODS + 2 * KT + k))
                        if mods:
                            mod_out(i * 2 + (5 * KT + k))
                    L.leave(KT // 2)

            def mlp(layer, mods):
                gate = layer * MODS + 5 * KT
                with dve.Fori(0, CHUNKS) as c:
                    L.enter(c, s=3 * HT, hid=HT, m=6 if mods else 0)
                    for k in range(2 * HT):
                        if k < HT:
                            dve.wait_ge(stage_done, L.count("s", 1))
                            dve.wait_ge(relu_done, L.count("hid", -1))
                            if k == 0:
                                dve.wait_ge(stage_free, L.count("s"))
                            else:
                                dve.wait_ge(hid_lo_done, L.count("hid"))
                            dve.scalar_tensor_tensor(cols3(tmp[1][:, 0:N]), stage_ps(L.at["s"]), 0.0,
                                                     cols3(tmp[0][:, 0:N]), ALU.max, ALU.mult).then_inc(stage_free, 1)
                            L.at["s"] += 1
                            dve.wait_ge(stage_free, L.count("s"))
                            dve.wait_ge(hid_hi_done, L.count("hid", -1))
                            dve.tensor_tensor(hid_lo[:, k, :], tmp[1][:, 0:N], hid_hi[:, k, :].bitcast(F32),
                                              ALU.subtract).then_inc(hid_lo_done, 1)
                            L.at["hid"] += 1
                        else:
                            for half in range(2):
                                j = (k - HT) * 2 + half
                                residual(j, gate + j)
                        if mods and k < 6:
                            mod_out(c * 6 + (MODS + k))
                    L.leave(CHUNKS)

            turn_out_(lambda b: dve.tensor_copy(mod_bias[:, :], ps[:, b:b + 2 * MODS]))
            turn_out_(lambda b: dve.tensor_copy(vec[:, :], ps[:, b:b + VROWS]))
            dve.wait_ge(cond_act, 1)
            own(dve.tensor_scalar(cond_tmp[:, :, :], cond_tmp[:, :, :], 1.0, None, ALU.add))
            own(dve.reciprocal(cond_tmp[:, :, :], cond_tmp[:, :, :]))
            for k, name in enumerate(("c", "c_ctx")):
                a, z = VEC[name]
                ins = dve.tensor_tensor(cond[:, :, k], cond_tmp[:, :, k], vec[:, a:z], ALU.mult)
            ins.then_inc(cond_ready, 1)
            for t in range(NT):
                for g in range(2):
                    turn_out_(lambda b: dve.tensor_copy(x[:, 4 * g:4 * g + 4, t * P:(t + 1) * P],
                                                        ps[:, b:b + 4 * P].rearrange("p (k n) -> p k n", k=4)))
            for m in range(FIRST_MODS):
                mod_out(m)
            norm(0, 0)

            pad = tmp[1]
            dve.wait_ge(h_lo_done, C["h"])
            for c in (0, NS + 1, NS + 2, N + 3):
                ins = dve.memset(pad[:, c:c + 1], 0.0)
            own(ins)
            taps, bias0 = VEC["conv_w"][0], VEC["conv_b"][0]
            W2 = N + 2
            with dve.Fori(0, KT // 2) as i:
                L.enter(i, s=6, m=6)
                S.enter(i, n=6)
                for f in range(2):
                    L.at["s"] += 1
                    mod_out(i * 6 + (FIRST_MODS + 3 * f))
                    dve.wait_ge(stage_done, L.count("s", 1))
                    dve.wait_ge(stage_free, L.count("s"))
                    dst = [pad[:, 1:1 + 2 * TB].rearrange("p (t n) -> p t n", t=2),
                           pad[:, 1 + 2 * TB:1 + NS], pad[:, NS + 3:N + 3]]
                    for o, (v, g, _) in zip(dst, parts(L.at["s"], tmp[0])):
                        ins = dve.tensor_tensor(o, v, g, ALU.mult)
                    ins.then_inc(stage_free, 1)
                    L.at["s"] += 1
                    mod_out(i * 6 + (FIRST_MODS + 3 * f + 1))
                    dve.wait_ge(stage_free, L.count("s"))
                    col = [vec[:, ds(i * 2 + (taps + w * KT + f), 1)] for w in range(3)]
                    own(dve.tensor_scalar(tmp[2][:, 0:W2], pad[:, 0:W2], col[0],
                                          vec[:, ds(i * 2 + (bias0 + f), 1)], ALU.mult, ALU.add))
                    for w in (1, 2):
                        own(dve.scalar_tensor_tensor(tmp[2][:, 0:W2], pad[:, w:w + W2], col[w], tmp[2][:, 0:W2],
                                                     ALU.mult, ALU.add))
                    dve.wait_ge(stage_done, L.count("s", 1))
                    out = v32[:, ds(i * 2 + f, 1), :].rearrange("p a n -> p (a n)")
                    cv = [tmp[2][:, 0:2 * TB].rearrange("p (t n) -> p t n", t=2), tmp[2][:, 2 * TB:NS],
                          tmp[2][:, NS + 2:W2]]
                    for c, (v, o, _) in zip(cv, parts(L.at["s"], out)):
                        ins = dve.tensor_tensor(o, v, c, ALU.mult)
                    ins.then_inc(stage_free, 1)
                    L.at["s"] += 1
                    mod_out(i * 6 + (FIRST_MODS + 3 * f + 2))
                S.leave(KT // 2)
                L.leave(KT // 2)
            low_rows(h_lo, v32, h_hi, KT)
            out_blocks(0, True)
            norm(0, 1)
            mlp(0, True)
            if LAYERS > 1:
                norm(1, 0)
                for dst in [ql[:, j, :] for j in range(QT)] + [ckv[:, j, 0:N] for j in range(CT)] + [kpe_t[:, :]]:
                    dve.wait_ge(stage_done, L.at["s"] - 1)
                    dve.tensor_copy(cols3(dst), stage_ps(L.at["s"])).then_inc(stage_free, 1)
                    L.at["s"] += 1
                turn_out_(lambda b: dve.tensor_copy(ckv[:, :, N:KEYS], ps[:, b:b + CT * P].rearrange(
                    "p (k n) -> p k n", k=CT)))
                for a, z in groups(NT, 4):
                    turn_out_(lambda b: dve.tensor_copy(kpe[:, a:z, :], ps[:, b:b + (z - a) * P].rearrange(
                        "p (k n) -> p k n", k=z - a)[:, :, P - ROPE:P]))

                def latent_norm(t, n, cols, g0, hi, lo):
                    add_squares(n)
                    C["rstd"] += 1
                    dve.wait_ge(rstd_done, C["rstd"])
                    L.at["s"] += 1
                    for j in range(n):
                        dve.scalar_tensor_tensor(t[:, j, 0:N], t[:, j, 0:N], vec[:, g0 + j:g0 + j + 1], rstd[:, :],
                                                 ALU.mult, ALU.mult).then_inc(t_done, 1)
                        C["t"] += 1
                    dve.wait_ge(t_done, C["t"])
                    low_rows(lo, t, hi, n)

                latent_norm(ql, QT, N, VEC["q_norm_g"][0], ql_hi, ql_lo)
                latent_norm(ckv, CT, KEYS, VEC["kv_norm_g"][0], ckv_hi, ckv_lo)
                turn_out_(lambda b: dve.tensor_copy(ckv_out[:, :], ps[:, b:b + KVR]))

                dve.wait_ge(gains_in, 16 * 4)
                dve.wait_ge(turn_out, C["turn"])

                def halves(ap):
                    return ap.rearrange("p t (a s d) -> p t a s d", a=2, s=2)

                def gains(g, tiles):
                    return g[:, NOPE:QK].unsqueeze(1).to_broadcast([P, tiles, ROPE])

                dve.tensor_tensor(rot_cos[:, :, :], trig[:, 0, :, :], gains(g_q, NT), ALU.mult)
                for s in range(2):
                    ins = dve.tensor_tensor(halves(rot_sin[:, :, :])[:, :, :, s, :], halves(trig[:, 1, :, :])[:, :, :, s, :],
                                            halves(gains(g_q, NT))[:, :, :, 1 - s, :], ALU.mult)
                dve.tensor_tensor(g_qk[:, :], g_q[:, 0:NOPE], g_k[:, 0:NOPE], ALU.mult)
                own(dve.tensor_tensor(kpe_rot[:, :, :], kpe[:, :, :], gains(g_k, KTILES), ALU.mult))
                dve.tensor_tensor(rot_a[:, :, :], kpe_rot[:, 0:NT, :], trig[:, 0, :, :], ALU.mult)
                for s in range(2):
                    ins = dve.tensor_tensor(halves(rot_b[:, :, :])[:, :, :, s, :],
                                            halves(kpe_rot[:, 0:NT, :])[:, :, :, 1 - s, :],
                                            halves(trig[:, 1, :, :])[:, :, :, s, :], ALU.mult)
                own(ins)
                own(dve.tensor_tensor(kpe_rot[:, 0:NT, :], rot_a[:, :, :], rot_b[:, :, :], ALU.add))
                dve.wait_ge(arena_ready, 3)
                for t in range(KTILES):
                    ins = dve.tensor_tensor_reduce(junk[:, :, :].rearrange("p a n -> p (a n)")[:, t * ROPE:(t + 1) * ROPE],
                                                   kpe[:, t, :], kpe[:, t, :], 1.0, 0.0, ALU.mult,
                                                   ALU.add, kpe_sq[:, t:t + 1])
                own(ins)
                dve.wait_ge(new_stored, 32)

                A = Place(j=0, u=0, g=0, m=0, r=0)

                def unit_out(ins):
                    ins.then_inc(unit_free, 1)
                    A.at["u"] += 1

                def unit_low(out, in_, hi):
                    A.at["hi"] += 1
                    dve.wait_ge(unit_hi, A.count("hi"))
                    unit_out(dve.tensor_tensor(out, in_, hi.bitcast(F32), ALU.subtract))

                A.at["hi"] = 0

                def v_units(k):
                    for a, z in groups(KTILES, 4):
                        b0 = unit_ps(k)
                        unit_low(v_cols(v_lo, a, z), ps[:, b0:b0 + (z - a) * 2 * VD].rearrange(
                            "p (t h n) -> p t h n", h=2, n=VD), v_cols(v_hi, a, z))
                        k += 1

                def turn_units(k, s):
                    for hi, lo, tiles in ((qT_hi[s], qT_lo[s], NT), (kT_hi[s], kT_lo[s], KTILES)):
                        for a, z in groups(tiles, 4):
                            b0 = unit_ps(k)
                            unit_low(lo[0:QK, a * P:z * P], ps[0:QK, b0:b0 + (z - a) * P], hi[0:QK, a * P:z * P])
                            k += 1

                def qk_units(k):
                    for a, z in groups(NT, 2):
                        dve.wait_ge(unit_done, A.count("u", -1))
                        b0 = unit_ps(k)
                        unit_out(dve.tensor_copy(q_tok[:, a:z, :, :].rearrange("p t h n -> p (t h n)"),
                                                 ps[:, b0:b0 + (z - a) * 2 * QK]))
                        k += 1
                    for a, z in groups(KTILES, 4):
                        dve.wait_ge(unit_done, A.count("u", -1))
                        b0 = unit_ps(k)
                        unit_out(dve.tensor_copy(k_tok[:, a:z, :, 0:NOPE], ps[:, b0:b0 + (z - a) * 2 * NOPE].rearrange(
                            "p (t h n) -> p t h n", h=2, n=NOPE)))
                        k += 1

                def squares(lo, hi):
                    for i in range(lo, min(hi, 2 * NT + 2 * KTILES)):
                        if i < 2 * NT:
                            row = q_tok[:, i // 2, i % 2, :]
                        else:
                            row = k_tok[:, (i - 2 * NT) // 2, i % 2, 0:NOPE]
                        n = QK if i < 2 * NT else NOPE
                        ins = dve.tensor_tensor_reduce(junk[:, i - lo, 0:n], row, row, 1.0, 0.0, ALU.mult, ALU.add,
                                                       ssq[:, i:i + 1])
                    own(ins)

                def squares_end():
                    squares(4 * NT, 2 * NT + 2 * KTILES)
                    k = ssq[:, 2 * NT:].rearrange("p (t h) -> p t h", h=2)
                    dve.tensor_tensor(k, k, kpe_sq[:, :].unsqueeze(2).to_broadcast([P, KTILES, 2]),
                                      ALU.add).then_inc(ssq_done, 1)

                def rotate_and_scale():
                    for h in range(2):
                        qr = q_tok[:, :, h, NOPE:QK]
                        dve.tensor_tensor(rot_a[:, :, :], qr, rot_cos[:, :, :], ALU.mult)
                        for s in range(2):
                            ins = dve.tensor_tensor(halves(rot_b[:, :, :])[:, :, :, s, :], halves(qr)[:, :, :, 1 - s, :],
                                                    halves(rot_sin[:, :, :])[:, :, :, s, :], ALU.mult)
                        own(ins)
                        own(dve.tensor_tensor(qr, rot_a[:, :, :], rot_b[:, :, :], ALU.add))
                    kn = k_tok[:, :, :, 0:NOPE].rearrange("p t h n -> p (t h) n")
                    own(dve.tensor_tensor(kn, kn, g_qk[:, :].unsqueeze(1).to_broadcast([P, 2 * KTILES, NOPE]), ALU.mult))
                    A.at["r"] += 1
                    dve.wait_ge(r_done, A.count("r"))
                    q = q_tok[:, :, :, :].rearrange("p t h n -> p (t h) n")
                    dve.tensor_tensor(q, q, r_tok[:, 0:2 * NT].unsqueeze(2).to_broadcast([P, 2 * NT, QK]), ALU.mult)
                    rk = r_tok[:, 2 * NT:]
                    dve.tensor_tensor(kn, kn, rk.unsqueeze(2).to_broadcast([P, 2 * KTILES, NOPE]), ALU.mult)
                    rk2 = rk.rearrange("p (t h) -> p t h", h=2)
                    for h in range(2):
                        ins = dve.tensor_tensor(k_tok[:, :, h, NOPE:QK], kpe_rot[:, :, :],
                                                rk2[:, :, h].unsqueeze(2).to_broadcast([P, KTILES, ROPE]), ALU.mult)
                    ins.then_inc(tok_ready, 1)

                def max_out(t):
                    n = NP if t == NT - 1 else NS + P
                    dve.wait_ge(max_mm, A.count("m", -1))
                    dve.tensor_reduce(row_max[:, t:t + 1], ps[:, 0:n], AX_X, ALU.max).then_inc(max_free, 1)
                    A.at["m"] += 1

                def max_rows(k, s):
                    dve.wait_ge(unit_done, A.count("u", -1))
                    b0 = unit_ps(k)
                    unit_out(dve.scalar_tensor_tensor(
                        qT_hi[s][QK:QROWS, :].rearrange("r (t n) -> r t n", n=P),
                        ps[0:NT, b0:b0 + P].unsqueeze(1).to_broadcast([NT, NT, P]), -1.0,
                        ident[0:NT, 0:NT].unsqueeze(2).to_broadcast([NT, NT, P]), ALU.mult, ALU.mult))

                def output(head, qb, p):
                    g = head * 3 + qb
                    n = NP if qb == 2 else BANK
                    r = slice(head * VD, head * VD + VD)
                    A.at["g"] += 1
                    dve.wait_ge(inv_done, A.count("g"))
                    o = o32[r, ds(p, 1), qb * BANK:qb * BANK + n].rearrange("p a n -> p (a n)")
                    dve.tensor_tensor(o, ps[r, (5 + g % 2) * BANK:(5 + g % 2) * BANK + n], inv[g % 2][r, 0:n],
                                      ALU.mult).then_inc(o_free, 1)

                def pair(last, p):
                    v_units(0)
                    turn_units(U_V, 1)
                    if not last:
                        qk_units(U_V + U_TURN)
                        dve.wait_ge(unit_free, A.count("u"))
                    for t in range(NT):
                        max_out(t)
                        if not last:
                            squares(4 * t, 4 * t + 4)
                    if not last:
                        squares_end()
                    max_rows(U_V + U_TURN + U_QK, 1)
                    output(0, 0, p)
                    if not last:
                        rotate_and_scale()
                    output(0, 1, p)
                    output(0, 2, p)
                    if not last:
                        turn_units(U_V + U_TURN + U_QK + U_MAX, 0)
                        for t in range(NT):
                            if t == 4:
                                output(1, 0, p)
                            max_out(t)
                    else:
                        output(1, 0, p)
                    if not last:
                        max_rows(U_V + U_TURN + U_QK + U_MAX + U_TURN, 0)
                    output(1, 1, p)
                    output(1, 2, p)

                qk_units(0)
                dve.wait_ge(unit_free, A.count("u"))
                for t in range(NT):
                    squares(4 * t, 4 * t + 4)
                squares_end()
                rotate_and_scale()
                turn_units(U_QK, 0)
                for t in range(NT):
                    max_out(t)
                max_rows(U_QK + U_TURN, 0)
                with dve.Fori(0, PAIRS - 1) as p:
                    A.enter(p, u=U_PAIR, g=6, m=2 * NT, r=1, hi=U_V + 2 * U_TURN)
                    S.enter(p, n=NT + 6)
                    pair(False, p)
                    S.leave(PAIRS - 1)
                    A.leave(PAIRS - 1)
                pair(True, PAIRS - 1)
                dve.wait_ge(o_free, 2 + 3 * HEADS)
                low_rows(h_lo, o32, h_hi, KT)
                dve.wait_ge(x_back, 16)
                out_blocks(1, False)
                norm(1, 1)
                mlp(1, False)
            dve.wait_ge(stage_free, L.at["s"])
            for t in range(NT):
                for g in range(2):
                    turn_out_(lambda b: dve.tensor_copy(y_out[:, t, 4 * g * P:4 * (g + 1) * P], ps[:, b:b + 4 * P]))


def groups(n, size):
    return [(a, min(a + size, n)) for a in range(0, n, size)]


def v_cols(t, a, z):
    return t[:, a:z, :].rearrange("p t (g n) -> p t g n", g=3)[:, :, 0:3:2, :]


def constants():
    import numpy as np
    grid_w, axis, theta = 64, ROPE // 2, np.float32(10000.0)
    pos = np.arange(NS)
    inv = np.power(theta, -np.arange(0, axis, 2, dtype=np.float32) / np.float32(axis)).astype(np.float32)
    trig = np.zeros((P, 2, NT, ROPE), np.float32)
    trig[:, 0] = 1.0
    for a, where in enumerate((pos // grid_w, pos % grid_w)):
        angle = where.astype(np.float32)[:, None] * inv[None]
        for s in range(2):
            cols = slice(a * axis + s * axis // 2, a * axis + (s + 1) * axis // 2)
            trig[:, 0, :NS // P, cols] = np.cos(angle).reshape(NS // P, P, -1).transpose(1, 0, 2)
            trig[:, 1, :NS // P, cols] = (np.sin(angle) * (2 * s - 1)).reshape(NS // P, P, -1).transpose(1, 0, 2)
    return {"ident": np.eye(P, dtype=np.float32), "trig": trig}


_INS = ["x_prompt", "x_sample", "cache_ckv", "cache_kpe", "c", "c_ctx", "norm1_g", "norm2_g", "mod_w", "mod_b",
        "mlp_w1", "mlp_w2", "sc_w_in", "sc_conv_w", "sc_conv_b", "sc_w_out", "mla_w_dq", "mla_q_norm_g",
        "mla_w_uq", "mla_w_dkv", "mla_kv_norm_g", "mla_w_ukv", "mla_qn_g", "mla_kn_g", "mla_w_o"]
_OUTS = [((1, NP, D), "float32"), ((1, NS, D), "float32"), ((1, 1, NP, KVR), "float32"), ((1, 1, NP, ROPE), "float32")]


def kernel(**inputs):
    import numpy as _np
    import concourse.bacc as _bacc
    from concourse.bass_utils import run_bass_kernel_spmd as _run

    nc = _bacc.Bacc("TRN2", target_bir_lowering=False, num_devices=1)
    arrays, tensors, outs = {}, {}, []
    data = {name: inputs[name] for name in _INS}
    data.update(constants())
    for name, a in data.items():
        a = _np.ascontiguousarray(a)
        arrays[f"in_{name}_dram"] = a
        tensors[name] = nc.dram_tensor(f"in_{name}_dram", a.shape, mybir.dt.from_np(a.dtype), kind="ExternalInput").ap()
    for i, (shape, dtype) in enumerate(_OUTS):
        outs.append(nc.dram_tensor(f"out_{i}_dram", shape, mybir.dt.from_np(_np.dtype(dtype)), kind="ExternalOutput").ap())
    build(nc, tensors, outs)
    r = _run(nc, [arrays], core_ids=[0])
    return tuple(r.results[0][f"out_{i}_dram"] for i in range(len(_OUTS)))
```

```python
from contextlib import ExitStack

import concourse.bass as bass
from concourse import mybir
from concourse.alu_op_type import AluOpType as ALU

ACT = mybir.ActivationFunctionType
AX_X = mybir.AxisListType.X
F32 = mybir.dt.float32
F32R = mybir.dt.float32r
ds = bass.ds

P = 128
D = 1024
KT = D // P
NS, NP = 1024, 128
N = NS + NP
NT = N // P
TB = 384
BANK = 512
FF = 4 * D
HT = 4
CHUNKS = FF // (HT * P)
MODS = 6 * KT
FIRST_MODS = 2 * KT
MOD_SLOTS = 8
EPS = 1e-6
HEADS, NOPE, ROPE, QK, VD = 16, 64, 32, 96, 64
QR, KVR = 384, 256
QT, CT = QR // P, KVR // P
KEYS = N + 128
KTILES = KEYS // P
PROMPT_K, CACHE_K = 8, 9
PAIRS = HEADS // 2
AUG = NT
QROWS = QK + AUG
SCALE = float(QK) ** -0.5
WSLOT = 1024
LAYERS = 2
STEPS = 19
STEP = [(k, q * 512, 512, q) for q in range(2) for k in (0, 1, 2, 3, 4, 5, 6, 7, CACHE_K)] + [(PROMPT_K, NS, NP, 2)]
PR = 3
LAG = 3
SPLIT_AT = 4
TURN_A = STEPS + 1
MAX_B, MAX_A = 0, TURN_A + 2
ROWS_B, ROWS_A = MAX_B + 13, MAX_A + 13
MLP_MODS = (0, 2, 3, 4, 5, 6)
SKEW = 2
TURNS = 2 + 2 * NT + (1 + 3 + 1 if LAYERS > 1 else 0) + 2 * NT

BLOCKS_IN, BLOCKS_OUT, BLOCKS_CHUNK = 3 * KT, KT, 2 * HT
MLP_BLOCKS = CHUNKS * BLOCKS_CHUNK
B_IN = 0
B_OUT = B_IN + BLOCKS_IN
B_MLP0 = B_OUT + BLOCKS_OUT
B_LAT = B_MLP0 + MLP_BLOCKS
B_ATT = B_LAT + QT + CT + 1
B_WO = B_ATT + 2 * PAIRS
B_MLP1 = B_WO + BLOCKS_OUT
B_END = B_MLP1 + MLP_BLOCKS

VEC = {}
_row = 0
for _name, _rows in (("norm1_g", 2 * KT), ("norm2_g", 2 * KT), ("conv_w", 3 * KT), ("conv_b", KT),
                     ("c", KT), ("c_ctx", KT), ("q_norm_g", QT), ("kv_norm_g", CT)):
    VEC[_name] = (_row, _row + _rows)
    _row += _rows
VROWS = _row


def block_dmas(b):
    if B_ATT <= b <= B_WO:
        return 3 if (b - B_ATT) % 2 == 0 else 2
    return 1


def block_words(b):
    if B_ATT <= b < B_WO:
        return QT * 2 * QK + CT * 2 * NOPE if (b - B_ATT) % 2 == 0 else CT * 2 * VD
    return WSLOT


def raw_loaded(b):
    return 16 * sum(block_dmas(k) for k in range(b % 2, b + 1, 2))


def block_stages(b):
    if B_ATT <= b < B_WO:
        return 0
    for start in (B_MLP0, B_MLP1):
        if start <= b < start + MLP_BLOCKS:
            return 1 if (b - start) % BLOCKS_CHUNK < HT else 2
    return 1


NORM_STAGES = {B_IN: 1, B_MLP0: 1, B_LAT: 1, B_LAT + QT + 1: 1, B_ATT: 1, B_MLP1: 1}


def stages_through(b):
    return sum(block_stages(k) for k in range(0, b + 1)) + sum(n for k, n in NORM_STAGES.items() if k <= b)


U_V, U_TURN, U_QK, U_MAX = 3, 6, 8, 1
U_PAIR = U_V + U_TURN + U_QK + U_MAX + U_TURN + U_MAX
U_LEAD = U_QK + U_TURN + U_MAX


def attention_released(b):
    p, odd = divmod(b - B_ATT, 2)
    if odd:
        return U_LEAD + p * U_PAIR + U_V
    return U_QK if p == 0 else U_LEAD + (p - 1) * U_PAIR + U_V + U_TURN + U_QK


class Place:

    def __init__(self, **at):
        self.at, self.step, self.i = dict(at), {}, None

    def enter(self, i, **step):
        self.i, self.step, self.entered = i, step, dict(self.at)

    def leave(self, turns):
        for k, n in self.step.items():
            assert self.at[k] - self.entered[k] == n, (k, self.at[k] - self.entered[k], n)
            self.at[k] = self.entered[k] + n * turns
        for k in self.at:
            assert k in self.step or self.at[k] == self.entered[k], k
        self.i, self.step = None, {}

    def count(self, key, back=0, f=lambda n: n):
        n = self.at[key] - back
        v = f(n)
        if self.i is None or not self.step.get(key):
            return v
        return self.i * (f(n + self.step[key]) - v) + v


def build(nc, T, outs):
    y_prompt, y_sample, new_ckv, new_kpe = outs
    with ExitStack() as ctx:
        def sem(name):
            return ctx.enter_context(nc.semaphore(name))

        cursor = [(nc.sbuf_base + 31) // 32 * 32]

        def at(name, shape, dt, offset):
            return nc.alloc_sbuf_tensor_at(name, shape, dt, offset=offset)

        def new(name, shape, dt=F32):
            words = 1
            for n in shape[1:]:
                words *= n
            t = at(name, shape, dt, cursor[0])
            cursor[0] += (words * 4 + 31) // 32 * 32
            return t

        ident = new("ident", [P, P])
        ones = new("ones", [P, P])
        trig = new("trig", [P, 2, NT, ROPE])
        eps = new("eps", [P, 1])
        vec = new("vec", [P, VROWS])
        mod_bias = new("mod_bias", [P, 2 * MODS])
        mod = new("mod", [P, 2 * MODS, 2])
        cond = new("cond", [P, KT, 2])
        cond_tmp = new("cond_tmp", [P, KT, 2])
        gain = new("gain", [P, 4, KT, 2])
        root = new("root", [P, NT])
        rstd = new("rstd", [P, N])
        rot_cos, rot_sin, rot_a, rot_b = (
            at(f"rot{k}", [P, NT, ROPE], F32, cursor[0] - N * 4 + k * NT * ROPE * 4) for k in range(4))
        kpe = new("kpe", [P, KTILES, ROPE])
        kpe_rot = new("kpe_rot", [P, KTILES, ROPE])
        kpe_sq = new("kpe_sq", [P, KTILES])
        g_q = new("g_q", [P, QK])
        g_k = new("g_k", [P, QK])
        g_qk = new("g_qk", [P, NOPE])

        w_raw = [new(f"w_raw{s}", [P, WSLOT]) for s in range(2)]
        w_hi = [new(f"w_hi{s}", [P, WSLOT], F32R) for s in range(2)]
        w_lo = [new(f"w_lo{s}", [P, WSLOT], F32R) for s in range(2)]

        G0 = cursor[0]
        v32 = new("v32", [P, KT, N])
        hid_hi = at("hid_hi", [P, HT, N], F32R, G0)
        hid_lo = at("hid_lo", [P, HT, N], F32R, G0 + HT * N * 4)
        mod_first = at("mod_first", [P, MOD_SLOTS, WSLOT], F32, G0)
        ql = at("ql", [P, QT, N], F32, G0)
        ckv = at("ckv", [P, CT, KEYS], F32, G0 + QT * N * 4)
        kpe_t = at("kpe_t", [P, N], F32, G0 + QT * N * 4 + CT * KEYS * 4)
        cache_in = at("cache_in", [P, KVR], F32, G0 + (QT + 1) * N * 4 + CT * KEYS * 4)
        ckv_out = at("ckv_out", [P, KVR], F32, G0 + (QT + 1) * N * 4 + CT * KEYS * 4 + KVR * 4)
        o32 = at("o32", [P, KT, N], F32, G0)

        H0 = cursor[0]
        h_hi = new("h_hi", [P, KT, N], F32R)
        h_lo = new("h_lo", [P, KT, N], F32R)
        x_in = at("x_in", [P, NT, D], F32, H0)
        vec_in = at("vec_in", [P, 2, P], F32, H0 + NT * D * 4)
        y_out = at("y_out", [P, NT, D], F32, H0)
        ql_hi = at("ql_hi", [P, QT, N], F32R, H0)
        ql_lo = at("ql_lo", [P, QT, N], F32R, H0 + QT * N * 4)
        ckv_hi = at("ckv_hi", [P, CT, KEYS], F32R, H0 + 2 * QT * N * 4)
        ckv_lo = at("ckv_lo", [P, CT, KEYS], F32R, H0 + 2 * QT * N * 4 + CT * KEYS * 4)
        A0 = H0 + 2 * QT * N * 4 + 2 * CT * KEYS * 4

        x = new("x", [P, KT, N])
        mod_raw = [new(f"mod_raw{s}", [P, WSLOT]) for s in range(2)]
        TW = N + 4
        tmp = [new(f"tmp{s}", [P, TW]) for s in range(4)]
        TOP = cursor[0]
        assert TOP <= nc.sbuf_usable_end, (TOP, nc.sbuf_usable_end)

        cursor[0] = A0
        q_tok = new("q_tok", [P, NT, 2, QK])
        k_tok = new("k_tok", [P, KTILES, 2, QK])
        v_hi = new("v_hi", [P, KTILES, 3 * VD], F32R)
        v_lo = new("v_lo", [P, KTILES, 3 * VD], F32R)
        qT_hi = [new(f"qT_hi{s}", [QROWS, N], F32R) for s in range(2)]
        qT_lo = [new(f"qT_lo{s}", [QROWS, N], F32R) for s in range(2)]
        kT_hi = [new(f"kT_hi{s}", [QROWS, KEYS], F32R) for s in range(2)]
        kT_lo = [new(f"kT_lo{s}", [QROWS, KEYS], F32R) for s in range(2)]
        p32, p_lo, p_hi = [], [], []
        for s in range(PR):
            p32.append(new(f"p32_{s}", [P, BANK]))
            p_lo.append(at(f"p_lo{s}", [P, BANK], F32R, cursor[0] - BANK * 4))
            p_hi.append(new(f"p_hi{s}", [P, BANK], F32R))
        sums = new("sums", [P, N])
        junk = new("junk", [P, 5, QK])
        ssq = new("ssq", [P, 2 * NT + 2 * KTILES])
        r_tok = new("r_tok", [P, 2 * NT + 2 * KTILES])
        row_max = new("row_max", [P, NT])
        assert cursor[0] <= nc.sbuf_usable_end

        ps = nc.alloc_psum_tensor("ps", [P, 8 * BANK], F32)

        def bank(k, n=BANK):
            return ps[:, k * BANK:k * BANK + n]

        def stage_ps(s):
            return ps[:, 3 * (s % 2) * BANK:3 * (s % 2 + 1) * BANK].rearrange("p (t n) -> p t n", t=3)[:, :, 0:TB]

        def mean_ps(s):
            b0 = (3 * (s % 2) + 2) * BANK + TB
            return ps[:, b0:b0 + NT]

        def parts(s, tile):
            v = stage_ps(s)
            return [(v[:, 0:2, :], tile[:, 0:2 * TB].rearrange("p (t n) -> p t n", t=2), 0),
                    (v[:, 2, 0:NS - 2 * TB], tile[:, 2 * TB:NS], 0),
                    (v[:, 2, NS - 2 * TB:TB], tile[:, NS:N], 1)]

        mod_prod = tmp[3][:, 0:WSLOT]
        mod_part = rstd[:, 0:2 * P].rearrange("p (c n) -> p c n", c=2)

        def cols3(tile):
            return tile.rearrange("p (t n) -> p t n", t=3)

        def unit_ps(k):
            return k % 3 * BANK

        def pv_ps(g, rows_, n):
            return ps[rows_, (5 + g % 3) * BANK:(5 + g % 3) * BANK + n]

        SEGS = ((0, NS, 0), (NS, N, 1))

        w_loaded = [sem(f"w_loaded{s}") for s in range(2)]
        m_loaded = [sem(f"m_loaded{s}") for s in range(2)]
        mf_loaded = [sem(f"mf_loaded{s}") for s in range(MOD_SLOTS)]
        x_loaded = [sem(f"x_loaded{s}") for s in range(3)]
        w_hi_done = sem("w_hi_done")
        w_lo_done = sem("w_lo_done")
        mod_mm = sem("mod_mm")
        mod_done = sem("mod_done")
        mod_product = sem("mod_product")
        mod_reduced = sem("mod_reduced")
        stage_done = sem("stage_done")
        stage_free = sem("stage_free")
        const_in = sem("const_in")
        gains_in = sem("gains_in")
        vec_loaded = sem("vec_loaded")
        turn_mm = sem("turn_mm")
        turn_out = sem("turn_out")
        cond_act = sem("cond_act")
        cond_ready = sem("cond_ready")
        sq_done = sem("sq_done")
        acc_done = sem("acc_done")
        mean_mm = sem("mean_mm")
        mean_root = sem("mean_root")
        mean_inverse = sem("mean_inverse")
        dve_self = sem("dve_self")
        t_done = sem("t_done")
        h_hi_done = sem("h_hi_done")
        h_lo_done = sem("h_lo_done")
        relu_done = sem("relu_done")
        hid_hi_done = sem("hid_hi_done")
        hid_lo_done = sem("hid_lo_done")
        y_stored = sem("y_stored")
        x_spilled = sem("x_spilled")
        x_back = sem("x_back")
        cache_loaded = sem("cache_loaded")
        new_stored = sem("new_stored")
        arena_ready = sem("arena_ready")
        unit_done = sem("unit_done")
        unit_hi = sem("unit_hi")
        unit_free = sem("unit_free")
        max_mm = sem("max_mm")
        max_free = sem("max_free")
        ssq_done = sem("ssq_done")
        r_root = sem("r_root")
        tok_ready = sem("tok_ready")
        s_mm = sem("s_mm")
        p_exp = sem("p_exp")
        p_hi_done = sem("p_hi_done")
        p_lo_done = sem("p_lo_done")
        p_free = sem("p_free")
        sums_used = sem("sums_used")
        o_free = sem("o_free")
        x_dram = nc.dram_tensor("x_spill", [P, KT, N], F32, kind="Internal").ap()

        def rows(ap):
            return ap.rearrange("(k p) n -> p k n", p=P)

        mod_v = [rows(T["mod_w"][l]) for l in range(2)]
        w1_v = [rows(T["mlp_w1"][l]) for l in range(2)]
        w2_v = [rows(T["mlp_w2"][l]) for l in range(2)]
        win_v, wout_v = rows(T["sc_w_in"][0]), rows(T["sc_w_out"][0])
        dq_v, dkv_v = rows(T["mla_w_dq"][0]), rows(T["mla_w_dkv"][0])
        uq_v, ukv_v = rows(T["mla_w_uq"][0]), rows(T["mla_w_ukv"][0])
        wo_v = rows(T["mla_w_o"][0])

        block = ctx.enter_context(nc.Block())

        @block.sync
        def _(sp):
            L = Place(b=0, m=FIRST_MODS)

            def load(*pieces):
                s = L.at["b"] % 2
                for piece in pieces:
                    sp.lower_ap_dma(piece[3])
                if L.i is not None or L.at["b"] >= 2:
                    sp.wait_ge(w_lo_done, L.count("b", 1))
                for off, kt, n, src in pieces:
                    dst = w_raw[s][:, off:off + kt * n].rearrange("p (k n) -> p k n", k=kt)
                    sp.dma_start(dst, src).then_inc(w_loaded[s], 16)
                L.at["b"] += 1

            def load_mod(l, col):
                s = L.at["m"] % 2
                src = mod_v[l][:, :, ds(col, P)]
                sp.lower_ap_dma(src)
                if L.i is not None or L.at["m"] >= FIRST_MODS + 2:
                    sp.wait_ge(mod_reduced, L.count("m", FIRST_MODS))
                sp.dma_start(mod_raw[s][:, :].rearrange("p (k n) -> p k n", k=KT), src).then_inc(m_loaded[s], 16)
                L.at["m"] += 1

            sp.dma_start(vec_in[0:2 * MODS, 0, :], T["mod_b"].rearrange("l (m p) -> (l m) p", p=P)).then_inc(vec_loaded, 16)
            for name, src in (("norm1_g", T["norm1_g"].rearrange("l (m p) -> (l m) p", p=P)),
                              ("norm2_g", T["norm2_g"].rearrange("l (m p) -> (l m) p", p=P)),
                              ("conv_w", T["sc_conv_w"].rearrange("l w (m p) -> (l w m) p", p=P)),
                              ("conv_b", T["sc_conv_b"].rearrange("l (m p) -> (l m) p", p=P)),
                              ("c", T["c"].rearrange("l (m p) -> (l m) p", p=P)),
                              ("c_ctx", T["c_ctx"].rearrange("(m p) -> m p", p=P)),
                              ("q_norm_g", T["mla_q_norm_g"].rearrange("l (m p) -> (l m) p", p=P)),
                              ("kv_norm_g", T["mla_kv_norm_g"].rearrange("l (m p) -> (l m) p", p=P))):
                a, z = VEC[name]
                sp.dma_start(vec_in[a:z, 1, :], src).then_inc(vec_loaded, 16)
            sp.dma_start(ident[:, :], T["ident"]).then_inc(const_in, 16)
            def load_first_mod(m):
                sp.dma_start(mod_first[:, m % MOD_SLOTS, :].rearrange("p (k n) -> p k n", k=KT),
                             mod_v[0][:, :, m * P:(m + 1) * P]).then_inc(mf_loaded[m % MOD_SLOTS], 16)

            for m in range(MOD_SLOTS):
                load_first_mod(m)
            xs = T["x_sample"][0].rearrange("(t p) n -> p t n", p=P)
            for g in range(2):
                sp.dma_start(x_in[:, 4 * g:4 * g + 4, :], xs[:, 4 * g:4 * g + 4, :]).then_inc(x_loaded[g], 16)
            sp.dma_start(x_in[:, NS // P, :], T["x_prompt"][0]).then_inc(x_loaded[2], 16)
            for m in range(MOD_SLOTS, FIRST_MODS):
                sp.wait_ge(mod_mm, m - MOD_SLOTS + 1)
                load_first_mod(m)
            sp.dma_start(trig[:, :, :, :], T["trig"]).then_inc(gains_in, 16)
            sp.dma_start(kpe[:, CACHE_K, :], T["cache_kpe"][0, 0]).then_inc(gains_in, 16)
            sp.dma_start(g_q[:, :], T["mla_qn_g"].to_broadcast([P, QK])).then_inc(gains_in, 16)
            sp.dma_start(g_k[:, :], T["mla_kn_g"].to_broadcast([P, QK])).then_inc(gains_in, 16)

            def load_in(f, m):
                for k, part in enumerate((1, 2, 0)):
                    load((0, KT, P, win_v[:, :, ds(f * P + part * D, P)]))
                    load_mod(0, m * P + k * P)

            load_in(0, FIRST_MODS)
            load_in(1, FIRST_MODS + 3)
            with sp.Fori(1, KT // 2) as i:
                L.enter(i - 1, b=6, m=6)
                for f in range(2):
                    load_in(i * 2 + f, i * 6 + (FIRST_MODS + 3 * f))
                L.leave(KT // 2 - 1)
            with sp.Fori(0, KT // 2) as i:
                L.enter(i, b=2, m=2)
                for j in range(2):
                    load((0, KT, P, wout_v[:, :, ds(i * 2 * P + j * P, P)]))
                    load_mod(0, i * 2 * P + (5 * KT + j) * P)
                L.leave(KT // 2)

            def load_mlp(l, mods):
                with sp.Fori(0, CHUNKS) as c:
                    L.enter(c, b=2 * HT, m=6 if mods else 0)
                    for k in range(2 * HT):
                        if k < HT:
                            load((0, KT, P, w1_v[l][:, :, ds(c * HT * P + k * P, P)]))
                        else:
                            load((0, HT, 2 * P, w2_v[l][:, ds(c * HT, HT), (k - HT) * 2 * P:(k - HT + 1) * 2 * P]))
                        if mods and k in MLP_MODS:
                            load_mod(1, c * 6 * P + MLP_MODS.index(k) * P)
                    L.leave(CHUNKS)

            load_mlp(0, True)
            if LAYERS > 1:
                for col in (0, P):
                    load((0, KT, P, dq_v[:, :, col:col + P]))
                sp.wait_ge(stage_done, stages_through(B_LAT - 1))
                sp.dma_start(cache_in[:, :], T["cache_ckv"][0, 0]).then_inc(cache_loaded, 16)
                load((0, KT, P, dq_v[:, :, 2 * P:3 * P]))
                for col in (0, P, KVR + ROPE - P):
                    load((0, KT, P, dkv_v[:, :, col:col + P]))
                with sp.Fori(0, PAIRS) as p:
                    L.enter(p, b=2)
                    load((0, QT, 2 * QK, uq_v[:, :, ds(p * 2 * QK, 2 * QK)]),
                         *[(QT * 2 * QK + h * CT * NOPE, CT, NOPE, ukv_v[:, :, ds(p * 256 + h * 128, NOPE)])
                           for h in range(2)])
                    load(*[(h * CT * VD, CT, VD, ukv_v[:, :, ds(p * 256 + (h * 128 + NOPE), VD)]) for h in range(2)])
                    L.leave(PAIRS)
                load(*[(a * P, z - a, P, wo_v[:, a:z, 0:P]) for a, z in ((0, 3), (3, 6), (6, KT))])
                load((0, KT, P, wo_v[:, :, P:2 * P]))
                sp.wait_ge(sums_used, 3 + 3 * PAIRS)
                sp.dma_start(x[:, :, :], x_dram).then_inc(x_back, 16)
                with sp.Fori(1, KT // 2) as i:
                    L.enter(i - 1, b=2)
                    for j in range(2):
                        load((0, KT, P, wo_v[:, :, ds(i * 2 * P + j * P, P)]))
                    L.leave(KT // 2 - 1)
                load_mlp(1, False)
            for t in range(NT):
                sp.wait_ge(turn_out, TURNS - 2 * NT + 2 * t + 2)
                dst = y_prompt[0] if t == NT - 1 else y_sample[0, t * P:(t + 1) * P, :]
                sp.dma_start(dst, y_out[:, t, :]).then_inc(y_stored, 16)
            sp.wait_ge(y_stored, 16 * NT)

        @block.gpsimd
        def _(pool):
            L = Place(b=0, m=FIRST_MODS)
            A = Place(j=0)
            pool.memset(ones[:, 0:P // 2], 1.0).then_inc(mod_reduced, 1)
            pool.memset(ones[:, P // 2:P], 1.0).then_inc(stage_free, 1)
            pool.memset(eps[:, :], EPS).then_inc(stage_free, 1)

            def split_lo(words=WSLOT):
                s = L.at["b"] % 2
                pool.wait_ge(w_hi_done, L.count("b", -1))
                pool.tensor_tensor(w_lo[s][:, 0:words], w_raw[s][:, 0:words], w_hi[s][:, 0:words].bitcast(F32),
                                   ALU.subtract).then_inc(w_lo_done, 1)
                L.at["b"] += 1

            def split_pairs(n):
                with pool.Fori(0, n) as i:
                    L.enter(i, b=2)
                    split_lo()
                    split_lo()
                    L.leave(n)

            def p_low(head, j):
                n = NP if j == STEPS - 1 else BANK
                s = (head * STEPS + j) % PR
                pool.wait_ge(p_hi_done, A.count("j", -1))
                pool.tensor_tensor(p_lo[s][:, 0:n], p32[s][:, 0:n], p_hi[s][:, 0:n].bitcast(F32),
                                   ALU.subtract).then_inc(p_lo_done, 1)
                A.at["j"] += 1

            def mod_products():
                m = L.at["m"]
                raw = mod_raw[m % 2][:, :].rearrange("p (k n) -> p k n", k=KT)
                pool.wait_ge(m_loaded[m % 2], L.count("m", 0, lambda n: 16 * ((n - FIRST_MODS) // 2 + 1)))
                pool.wait_ge(mod_reduced, L.count("m", FIRST_MODS - 1))
                for c, out in enumerate((mod_prod.rearrange("p (k n) -> p k n", k=KT), raw)):
                    ins = pool.tensor_tensor(out, raw, cond[:, :, c:c + 1].to_broadcast([P, KT, P]), ALU.mult)
                ins.then_inc(mod_product, 1)
                L.at["m"] += 1

            def blocks(turns, n, mods):
                with pool.Fori(0, turns) as i:
                    L.enter(i, b=n, m=len(mods))
                    for k in range(n):
                        split_lo()
                        if k in mods:
                            mod_products()
                    L.leave(turns)

            pool.wait_ge(cond_ready, 1)
            blocks(KT // 2, 6, range(6))
            blocks(KT // 2, 2, range(2))
            blocks(CHUNKS, 2 * HT, MLP_MODS)
            if LAYERS > 1:
                split_pairs((B_ATT - B_LAT) // 2)
            if LAYERS > 1:
                split_lo(block_words(B_ATT))
                split_lo(block_words(B_ATT + 1))
                pool.wait_ge(h_lo_done, 4 * KT + QT + CT)
                pool.wait_ge(x_spilled, 16)
                done = {}
                for part, value, signal in ((v_hi[:, :, VD:2 * VD], 1.0, p_free), (v_lo[:, :, VD:2 * VD], 0.0, p_free),
                                            (qT_lo[0][QK:QROWS, :], 0.0, p_free),
                                            (qT_lo[1][QK:QROWS, :], 0.0, arena_ready),
                                            (kT_lo[0][QK:QROWS, :], 0.0, o_free), (kT_lo[1][QK:QROWS, :], 0.0, o_free),
                                            (kT_hi[0][QK:QROWS, :], 1.0, o_free),
                                            (kT_hi[1][QK:QROWS, :], 1.0, arena_ready)):
                    pool.memset(part.bitcast(F32), value).then_inc(signal, 1)
                    done[signal.name] = done.get(signal.name, 0) + 1
                    pool.wait_ge(signal, done[signal.name])
                split_lo(block_words(B_ATT))
                with pool.Fori(0, PAIRS - 1) as p:
                    L.enter(p, b=2)
                    A.enter(p, j=2 * STEPS)
                    for head in range(2):
                        for j in range(STEPS):
                            p_low(head, j)
                            if j == SPLIT_AT:
                                split_lo(block_words(B_ATT + 1) if head == 0 else WSLOT)
                    A.leave(PAIRS - 1)
                    L.leave(PAIRS - 1)
                for head in range(2):
                    for j in range(STEPS):
                        p_low(head, j)
                split_lo()
                split_pairs((B_END - B_WO - 2) // 2)

        @block.scalar
        def _(act):
            L = Place(b=0, s=2, hid=0, acc=0)
            C = dict(rms=0, t=0)
            A = Place(j=0, u=0, r=0, p=0)

            def split_hi(words=WSLOT):
                b = L.at["b"]
                s = b % 2
                act.wait_ge(w_loaded[s], L.count("b", 0, raw_loaded))
                if B_ATT <= b - 2 < B_WO:
                    act.wait_ge(unit_done, L.count("b", 2, attention_released))
                elif L.i is not None or b >= 2:
                    act.wait_ge(stage_done, L.count("b", 2, stages_through))
                act.activation(w_hi[s][:, 0:words], w_raw[s][:, 0:words], ACT.Copy).then_inc(w_hi_done, 1)
                L.at["b"] += 1

            def square(src, t, width):
                if L.i is not None or L.at["acc"] >= 2:
                    act.wait_ge(acc_done, L.count("acc", 1))
                act.activation(tmp[t][:, 0:N], src, ACT.Square, scale=width ** -0.5).then_inc(sq_done, 1)
                L.at["acc"] += 1

            def rms(src, n, width):
                for j in range(n):
                    square(src(j), j % 2, width)
                C["rms"] += 1
                act.wait_ge(mean_mm, C["rms"])
                act.activation(root[:, :], mean_ps(L.at["s"]), ACT.Sqrt, bias=eps[:, 0:1]).then_inc(mean_root, 1)
                act.wait_ge(stage_done, L.at["s"] - 1)
                act.activation(cols3(rstd[:, :]), stage_ps(L.at["s"]), ACT.Copy).then_inc(stage_free, 1)
                L.at["s"] += 1

            def norm(layer, which, sums=True):
                if sums:
                    rms(None, 0, D)
                shift = layer * MODS + 3 * which * KT
                for j in range(KT):
                    act.wait_ge(t_done, C["t"] + 1)
                    for a, z, c in SEGS:
                        ins = act.activation(h_hi[:, j, a:z], tmp[j % 2][:, a:z], ACT.Identity,
                                             bias=mod[:, shift + j, c:c + 1])
                    ins.then_inc(h_hi_done, 1)
                    C["t"] += 1

            def split_rows(src):
                for j in range(KT):
                    act.activation(h_hi[:, j, :], src[:, j, :], ACT.Copy).then_inc(h_hi_done, 1)

            def stream_square(j, t):
                act.wait_ge(stage_free, L.count("s"))
                square(x[:, ds(j, 1), :].rearrange("p a n -> p (a n)"), t, D)

            def out_blocks():
                with act.Fori(0, KT // 2) as i:
                    L.enter(i, b=2, s=2, acc=2)
                    for k in range(2):
                        split_hi()
                        L.at["s"] += 1
                        stream_square(i * 2 + k, k)
                    L.leave(KT // 2)

            def chunk(split_last=True, squares=False):
                for k in range(2 * HT):
                    if k < HT:
                        act.wait_ge(stage_done, L.count("s", 1))
                        act.activation(cols3(tmp[0][:, 0:N]), stage_ps(L.at["s"]), ACT.Relu).then_inc(relu_done, 1)
                        L.at["s"] += 1
                        act.wait_ge(stage_free, L.count("s"))
                        act.activation(hid_hi[:, k, :], tmp[1][:, 0:N], ACT.Copy).then_inc(hid_hi_done, 1)
                        L.at["hid"] += 1
                    else:
                        for half in range(2):
                            L.at["s"] += 1
                            if squares:
                                stream_square(2 * (k - HT) + half, half)
                    if split_last or k < 2 * HT - 2:
                        split_hi()

            def mlp(layer):
                with act.Fori(0, CHUNKS - 1) as c:
                    L.enter(c, b=2 * HT, s=3 * HT, hid=HT)
                    chunk()
                    L.leave(CHUNKS - 1)
                last = layer == LAYERS - 1
                chunk(not last, not last)

            act.wait_ge(turn_out, 2)
            for k, name in enumerate(("c", "c_ctx")):
                a, z = VEC[name]
                ins = act.activation(cond_tmp[:, :, k], vec[:, a:z], ACT.Exp, scale=-1.0)
            ins.then_inc(cond_act, 1)
            act.wait_ge(turn_out, 2 + 2 * NT)
            rms(lambda j: x[:, j, :], KT, D)
            split_hi()
            split_hi()
            norm(0, 0, False)

            def in_blocks():
                for k in range(6):
                    if k % 3 == 0:
                        act.wait_ge(stage_done, L.count("s", 1))
                        act.wait_ge(stage_free, L.count("s"))
                        act.activation(cols3(tmp[0][:, 0:N]), stage_ps(L.at["s"]), ACT.Copy).then_inc(stage_free, 1)
                    L.at["s"] += 1
                    split_hi()

            with act.Fori(0, KT // 2) as i:
                L.enter(i, b=6, s=6)
                in_blocks()
                L.leave(KT // 2)
            act.wait_ge(stage_free, L.at["s"])
            split_rows(v32)
            out_blocks()
            norm(0, 1)
            mlp(0)
            if LAYERS > 1:
                def latent_high(hi, t, n):
                    for j in range(n):
                        act.wait_ge(t_done, C["t"] + 1)
                        act.activation(hi[:, j, :], t[:, j, :], ACT.Copy).then_inc(h_hi_done, 1)
                        C["t"] += 1

                norm(1, 0)
                for k in range(QT + CT + 1):
                    split_hi(block_words(L.at["b"]))
                    L.at["s"] += 1
                    if k == 0:
                        act.wait_ge(h_lo_done, 4 * KT)
                        act.dma_start(x_dram, x[:, :, :]).then_inc(x_spilled, 16)
                    if k == QT - 1:
                        act.wait_ge(stage_free, L.at["s"])
                        for j in range(QT):
                            square(ql[:, j, :], j % 2, QR)
                    if k == QT:
                        rms(None, 0, QR)
                    if k == QT + CT - 1:
                        act.wait_ge(stage_free, L.at["s"])
                        for j in range(CT):
                            square(ckv[:, j, 0:N], j % 2, KVR)
                act.wait_ge(stage_done, L.at["s"] - 2)
                latent_high(ql_hi, ql, QT)
                rms(None, 0, KVR)
                latent_high(ckv_hi, ckv, CT)
                act.wait_ge(turn_out, TURNS - 2 * NT)
                act.dma_start(new_ckv[0, 0], ckv_out[:, :]).then_inc(new_stored, 16)
                act.dma_start(new_kpe[0, 0], kpe[:, PROMPT_K, :]).then_inc(new_stored, 16)

                def unit_high(out, in_):
                    act.wait_ge(unit_done, A.count("u", -1))
                    act.activation(out, in_, ACT.Copy).then_inc(unit_hi, 1)
                    A.at["u"] += 1

                def v_units(k):
                    for a, z in groups(KTILES, 4):
                        b0 = unit_ps(k)
                        unit_high(v_cols(v_hi, a, z), ps[:, b0:b0 + (z - a) * 2 * VD].rearrange(
                            "p (t h n) -> p t h n", h=2, n=VD))
                        k += 1

                def turn_units(k, s):
                    for dst, tiles in ((qT_hi[s], NT), (kT_hi[s], KTILES)):
                        for a, z in groups(tiles, 4):
                            b0 = unit_ps(k)
                            unit_high(dst[0:QK, a * P:z * P], ps[0:QK, b0:b0 + (z - a) * P])
                            k += 1

                def token_rstd():
                    act.wait_ge(ssq_done, A.count("r", -1))
                    act.activation(r_tok[:, :], ssq[:, :], ACT.Sqrt, bias=eps[:, 0:1]).then_inc(r_root, 1)
                    A.at["r"] += 1

                def step(head, j):
                    n = NP if j == STEPS - 1 else BANK
                    pos = head * STEPS + j
                    s = pos % PR
                    act.wait_ge(s_mm, A.count("j", -1))
                    act.wait_ge(p_free, A.count("j", 1 - PR if pos < 2 else -1))
                    act.activation(p32[s][:, 0:n], bank(3 + pos % 2, n), ACT.Exp, scale=SCALE).then_inc(p_exp, 1)
                    act.wait_ge(p_exp, A.count("j", -1))
                    act.activation(p_hi[s][:, 0:n], p32[s][:, 0:n], ACT.Copy).then_inc(p_hi_done, 1)
                    A.at["j"] += 1

                def output(head, qb, p):
                    n = NP if qb == 2 else BANK
                    g = head * 3 + qb
                    to, of = (slice(h * VD, h * VD + VD) for h in (head, 1 - head))
                    cols = slice(qb * BANK, qb * BANK + n)
                    done = PR + head * STEPS + (9, 18, 19)[qb]
                    act.wait_ge(p_free, A.count("p", 0, lambda n: 2 * STEPS * n + done))
                    if head == 0:
                        act.wait_ge(sums_used, A.count("p", 0, lambda n: 3 * n + qb + 1))
                    act.activation(o32[to, ds(p, 1), cols].rearrange("p a n -> p (a n)"), pv_ps(g, to, n), ACT.Copy)
                    act.activation(sums[to, cols], pv_ps(g, of, n), ACT.Copy).then_inc(o_free, 1)

                def pair(last, p):
                    for pos in range(2 * STEPS):
                        head, j = divmod(pos, STEPS)
                        step(head, j)
                        if pos == LAG - 2:
                            v_units(0)
                        if pos == LAG - 1:
                            turn_units(U_V, 1)
                            if not last:
                                A.at["u"] += U_QK
                        if pos == ROWS_B:
                            A.at["u"] += U_MAX
                        if pos == ROWS_B + 1 and not last:
                            token_rstd()
                        if pos == TURN_A + LAG and not last:
                            turn_units(U_V + U_TURN + U_QK + U_MAX, 0)
                            A.at["u"] += U_MAX
                        if j == SPLIT_AT and not last:
                            split_hi(block_words(B_ATT + 1) if head == 0 else WSLOT)
                        if pos in (17, STEPS + 9 + LAG):
                            output(head, 0, p)
                        if pos in (17 + LAG + 1, 18 + LAG + 1):
                            output(0, pos - 17 - LAG, p)
                    output(1, 1, p)
                    output(1, 2, p)
                    A.at["p"] += 1

                act.wait_ge(x_spilled, 16)
                A.at["u"] += U_QK
                token_rstd()
                turn_units(U_QK, 0)
                split_hi(block_words(B_ATT))
                A.at["u"] += U_MAX
                with act.Fori(0, PAIRS - 1) as p:
                    L.enter(p, b=2)
                    A.enter(p, j=2 * STEPS, u=U_PAIR, r=1, p=1)
                    pair(False, p)
                    A.leave(PAIRS - 1)
                    L.leave(PAIRS - 1)
                pair(True, PAIRS - 1)
                split_hi()
                act.wait_ge(sums_used, 3 + 3 * PAIRS)
                split_rows(o32)
                out_blocks()
                norm(1, 1)
                mlp(1)

        @block.tensor
        def _(pe):
            L = Place(b=0, s=2, m=0, hid=0)
            C = dict(turn=0, acc=0, h=0, rms=0)

            def three(outs, k, first, last, lhs, rhs):
                ins = None
                for n, (a, b) in enumerate(((0, 0), (0, 1), (1, 0))):
                    for out, cols in outs:
                        ins = pe.matmul(out, lhs[a], rhs[b](cols), start=first and n == 0, stop=last and n == 2)
                return ins

            def stage(w0, tiles, src, ready=None):
                s, slot = L.at["s"], L.at["b"] % 2
                pe.wait_ge(stage_free, L.count("s", 1))
                v = stage_ps(s)
                for k in range(tiles):
                    if ready:
                        ready(k)
                    w = w0(k)
                    ins = three([(v[:, t, :], t) for t in range(3)], k, k == 0, k == tiles - 1,
                                [w_hi[slot][:, w:w + P], w_lo[slot][:, w:w + P]],
                                [lambda t, r=r: r[:, k, t * TB:(t + 1) * TB] for r in src])
                ins.then_inc(stage_done, 1)
                L.at["s"] += 1

            def weights(ahead=0):
                pe.wait_ge(w_lo_done, L.count("b", -1 - ahead))

            def skewed_blocks(ready):
                for k in range(KT + SKEW):
                    for n in range(2):
                        t = k - n * SKEW
                        if not 0 <= t < KT:
                            continue
                        s, slot = L.at["s"] + n, (L.at["b"] + n) % 2
                        if t == 0:
                            weights(n)
                            pe.wait_ge(stage_free, L.count("s", 1 - n))
                        if n == 0:
                            ready(t)
                        v = stage_ps(s)
                        ins = three([(v[:, c, :], c) for c in range(3)], t, t == 0, t == KT - 1,
                                    [w_hi[slot][:, t * P:(t + 1) * P], w_lo[slot][:, t * P:(t + 1) * P]],
                                    [lambda c, h=h: h[:, t, c * TB:(c + 1) * TB] for h in (h_hi, h_lo)])
                        if t == KT - 1:
                            ins.then_inc(stage_done, 1)
                L.at["s"] += 2
                L.at["b"] += 2

            def h_block(ready=None):
                weights()
                stage(lambda k: k * P, KT, (h_hi, h_lo), ready)
                L.at["b"] += 1

            def h_ready(base):
                return lambda k: pe.wait_ge(h_lo_done, base + k + 1)

            def mod_tile(raw, loaded, count):
                b = 6 + L.at["m"] % 2
                pe.wait_ge(loaded, count)
                if L.at["m"] >= 2:
                    pe.wait_ge(mod_done, L.at["m"] - 1)
                for k in range(KT):
                    ins = pe.matmul(bank(b, 2), raw[:, k * P:(k + 1) * P], cond[:, k, :], start=k == 0, stop=k == KT - 1)
                ins.then_inc(mod_mm, 1)
                L.at["m"] += 1

            def mod_next():
                pe.wait_ge(mod_reduced, L.count("m", FIRST_MODS - 2))
                pe.wait_ge(mod_done, L.count("m", 1))
                b = 6 + L.at["m"] % 2
                for c in range(2):
                    ins = pe.matmul(ps[:, b * BANK + c:b * BANK + c + 1], mod_part[:, c, :], ones[:, 0:1],
                                    start=True, stop=True)
                ins.then_inc(mod_mm, 1)
                L.at["m"] += 1

            def turn(pieces, out_free):
                b = 6 + C["turn"] % 2
                if out_free > 0:
                    pe.wait_ge(turn_out, out_free)
                for k, (src, rows_) in enumerate(pieces):
                    ins = pe.transpose(ps[:, b * BANK + k * P:b * BANK + k * P + rows_], src, ident[0:rows_, 0:rows_])
                ins.then_inc(turn_mm, 1)
                C["turn"] += 1

            def sum_squares(n):
                s = L.at["s"]
                C["acc"] += n
                pe.wait_ge(acc_done, C["acc"])
                pe.wait_ge(stage_free, max(s - 1, 2))
                for t in range(NT):
                    ins = pe.matmul(mean_ps(s)[:, t:t + 1], tmp[2][:, t * P:(t + 1) * P], ones[:, 0:1],
                                    start=True, stop=True)
                ins.then_inc(mean_mm, 1)
                C["rms"] += 1
                pe.wait_ge(mean_inverse, C["rms"])
                for t in range(NT):
                    ins = pe.matmul(stage_ps(s)[:, t // 3, t % 3 * P:(t % 3 + 1) * P],
                                    root[:, t:t + 1].to_broadcast([P, P]), ident[:, :], start=True, stop=True)
                ins.then_inc(stage_done, 1)
                L.at["s"] += 1

            def chunk(mods, behind_norm=None):
                if behind_norm:
                    skewed_blocks(behind_norm)
                for k in range(2 * HT):
                    if k < HT:
                        if not (behind_norm and k < 2):
                            h_block()
                    else:
                        weights()
                        for half in range(2):
                            def hid_ready(t):
                                pe.wait_ge(hid_lo_done, L.count("hid", -t - 1))
                            stage(lambda t: t * 2 * P + half * P, HT, (hid_hi, hid_lo),
                                  hid_ready if k == HT and half == 0 else None)
                        L.at["b"] += 1
                    if mods and k in MLP_MODS:
                        mod_next()
                L.at["hid"] += HT

            def mlp(mods):
                chunk(mods, h_ready(C["h"]))
                with pe.Fori(1, CHUNKS) as c:
                    L.enter(c - 1, b=2 * HT, s=3 * HT, m=6 if mods else 0, hid=HT)
                    chunk(mods)
                    L.leave(CHUNKS - 1)

            pe.wait_ge(vec_loaded, 16 * 9)
            pe.wait_ge(const_in, 16)
            turn([(vec_in[0:2 * MODS, 0, :], 2 * MODS)], 0)
            turn([(vec_in[0:VROWS, 1, :], VROWS)], 0)

            def first_mods(lo, hi):
                for m in range(lo, hi):
                    mod_tile(mod_first[:, m % MOD_SLOTS, :], mf_loaded[m % MOD_SLOTS], 16 * (m // MOD_SLOTS + 1))

            pe.wait_ge(cond_ready, 1)
            pe.wait_ge(turn_out, C["turn"])
            first_mods(0, MOD_SLOTS)
            pe.wait_ge(mod_done, MOD_SLOTS)
            for t in range(NT):
                pe.wait_ge(x_loaded[t // 4], 16)
                for g in range(2):
                    turn([(x_in[:, t, (4 * g + k) * P:(4 * g + k + 1) * P], P) for k in range(4)], C["turn"] - 1)
            pe.wait_ge(turn_out, C["turn"])
            first_mods(MOD_SLOTS, MOD_SLOTS + KT // 2)
            sum_squares(KT)
            first_mods(MOD_SLOTS + KT // 2, FIRST_MODS)
            with pe.Fori(0, KT // 2) as i:
                L.enter(i, b=6, s=6, m=6)
                for k in range(6):
                    h_block(h_ready(0) if k == 0 else None)
                    mod_next()
                L.leave(KT // 2)
            C["h"] = KT

            def out_blocks(mods):
                with pe.Fori(0, KT // 2) as i:
                    L.enter(i, b=2, s=2, m=2 if mods else 0)
                    for k in range(2):
                        h_block(h_ready(C["h"]) if k == 0 else None)
                        if mods:
                            mod_next()
                    L.leave(KT // 2)
                C["h"] += KT

            out_blocks(True)
            sum_squares(KT)
            mlp(True)
            C["h"] += KT
            if LAYERS > 1:
                sum_squares(KT)
                skewed_blocks(h_ready(C["h"]))
                for k in range(2, QT + 1):
                    h_block()
                sum_squares(QT)
                for k in range(QT + 1, QT + CT):
                    h_block()
                pe.wait_ge(mod_done, 2 * MODS)
                pe.wait_ge(cache_loaded, 16)
                turn([(cache_in[:, k * P:(k + 1) * P], P) for k in range(CT)], C["turn"] - 1)
                h_block()
                C["h"] += KT
                sum_squares(CT)
                for a, z in groups(NT, 4):
                    turn([(kpe_t[:, t * P:(t + 1) * P], P) for t in range(a, z)], C["turn"] - 1)
                pe.wait_ge(t_done, 3 * KT + QT + CT)
                turn([(ckv[:, k, NS:N], P) for k in range(CT)], C["turn"] - 1)

                A = Place(j=0, u=0, g=0, m=0, tok=0)
                C["h"] += QT + CT
                pe.wait_ge(h_lo_done, C["h"])
                pe.wait_ge(stage_free, L.at["s"])

                def unit(k):
                    back = 0 if k == 0 else 2
                    if A.i is not None or A.at["u"] > back:
                        pe.wait_ge(unit_free, A.count("u", back))
                    return unit_ps(k)

                def unit_end(ins):
                    ins.then_inc(unit_done, 1)
                    A.at["u"] += 1

                def qk_units(k):
                    weights()
                    for a, z in groups(NT, 2):
                        b0 = unit(k)
                        for t in range(a, z):
                            out = ps[:, b0 + (t - a) * 2 * QK:b0 + (t - a + 1) * 2 * QK]
                            for kt in range(QT):
                                cols = slice(kt * 2 * QK, (kt + 1) * 2 * QK)
                                ins = three([(out, 0)], kt, kt == 0, kt == QT - 1,
                                            [r[:, kt, t * P:(t + 1) * P] for r in (ql_hi, ql_lo)],
                                            [lambda _, w=w: w[:, cols] for w in (w_hi[0], w_lo[0])])
                        unit_end(ins)
                        k += 1
                    kv_units(k, 0, QT * 2 * QK)

                def kv_units(k, slot, w0):
                    for a, z in groups(KTILES, 4):
                        b0 = unit(k)
                        for t in range(a, z):
                            out = ps[:, b0 + (t - a) * 2 * VD:b0 + (t - a + 1) * 2 * VD].rearrange(
                                "p (h n) -> p h n", h=2)
                            for kt in range(CT):
                                ins = three([(out, 0)], kt, kt == 0, kt == CT - 1,
                                            [r[:, kt, t * P:(t + 1) * P] for r in (ckv_hi, ckv_lo)],
                                            [lambda _, w=w: w[:, w0:w0 + 2 * CT * VD].rearrange(
                                                "p (h k n) -> p h k n", h=2, k=CT)[:, :, kt, :]
                                             for w in (w_hi[slot], w_lo[slot])])
                        unit_end(ins)
                        k += 1
                    L.at["b"] += 1

                def turn_units(k, head):
                    pe.wait_ge(tok_ready, A.count("tok"))
                    for src, tiles in ((q_tok, NT), (k_tok, KTILES)):
                        for a, z in groups(tiles, 4):
                            b0 = unit(k)
                            for t in range(a, z):
                                ins = pe.transpose(ps[0:QK, b0 + (t - a) * P:b0 + (t - a + 1) * P],
                                                   src[:, t, head, :], ident[:, :])
                            unit_end(ins)
                            k += 1

                def max_tile(s, t):
                    if t == 0:
                        pe.wait_ge(unit_free, A.count("u"))
                    if A.i is not None or A.at["m"] > 0:
                        pe.wait_ge(max_free, A.count("m"))
                    keys = [(PROMPT_K * P, P, 0)] if t == NT - 1 else [
                        (0, BANK, 0), (BANK, BANK, BANK), (CACHE_K * P, P, 2 * BANK)]
                    for c0, n, b0 in keys:
                        ins = pe.matmul(ps[:, b0:b0 + n], qT_hi[s][0:QK, t * P:(t + 1) * P],
                                        kT_hi[s][0:QK, c0:c0 + n], start=True, stop=True)
                    ins.then_inc(max_mm, 1)
                    A.at["m"] += 1

                def max_unit(k):
                    pe.wait_ge(max_free, A.count("m"))
                    b0 = unit(k)
                    unit_end(pe.transpose(ps[0:NT, b0:b0 + P], row_max[:, :], ident[:, :]))

                def scores(pos, ahead=LAG):
                    head, j = divmod(pos, STEPS)
                    kt, q0, n, _ = STEP[j]
                    if j == 0:
                        pe.wait_ge(unit_free, A.count("u"))
                    if ahead >= 2:
                        pe.wait_ge(p_exp, A.count("j", 1 - ahead))
                    ins = three([(bank(3 + pos % 2, n), 0)], 0, True, True,
                                [r[head][:, kt * P:(kt + 1) * P] for r in (kT_hi, kT_lo)],
                                [lambda _, r=r: r[head][:, q0:q0 + n] for r in (qT_hi, qT_lo)])
                    ins.then_inc(s_mm, 1)

                def values(pos):
                    head, j = divmod(pos, STEPS)
                    kt, _, n, qb = STEP[j]
                    g = head * 3 + qb
                    first, last = j in (0, 9, 18), j in (8, 17, 18)
                    if first:
                        pe.wait_ge(o_free, A.count("g", -1))
                    pe.wait_ge(p_lo_done, A.count("j", -1))
                    ins = three([(pv_ps(g, slice(0, P), n), 0)], 0, first, last,
                                [r[:, kt, head * VD:head * VD + P] for r in (v_hi, v_lo)],
                                [lambda _, r=r: r[pos % PR][:, 0:n] for r in (p_hi, p_lo)])
                    ins.then_inc(p_free, 1)
                    A.at["j"] += 1
                    if last:
                        A.at["g"] += 1

                def pair(last):
                    weights()
                    kv_units(0, 1, 0)
                    scores(LAG - 1, LAG - 1)
                    turn_units(U_V, 1)
                    if not last:
                        qk_units(U_V + U_TURN)
                        A.at["tok"] += 1
                    pe.wait_ge(unit_free, A.count("u", (0 if last else U_QK) + U_TURN))
                    def maxima(half):
                        for s, start in ((1, MAX_B), (0, MAX_A)):
                            t, off = divmod(half - 2 * start, 3)
                            if off == 0 and 0 <= t < NT and not (last and s == 0):
                                max_tile(s, t)

                    for pos in range(2 * STEPS):
                        if pos + LAG < 2 * STEPS:
                            scores(pos + LAG)
                        elif pos > 2 * STEPS - LAG and not last:
                            scores(pos - (2 * STEPS - LAG + 1), LAG - 1)
                        maxima(2 * pos)
                        values(pos)
                        maxima(2 * pos + 1)
                        if pos == ROWS_B:
                            max_unit(U_V + U_TURN + U_QK)
                        if not last:
                            k = U_V + U_TURN + U_QK + U_MAX
                            if pos == TURN_A:
                                turn_units(k, 0)
                            if pos == ROWS_A:
                                max_unit(k + U_TURN)

                qk_units(0)
                A.at["tok"] += 1
                pe.wait_ge(arena_ready, 2)
                turn_units(U_QK, 0)
                for t in range(NT):
                    max_tile(0, t)
                max_unit(U_QK + U_TURN)
                for pos in range(LAG - 1):
                    scores(pos, pos)
                with pe.Fori(0, PAIRS - 1) as p:
                    L.enter(p, b=2)
                    A.enter(p, j=2 * STEPS, u=U_PAIR, g=6, m=2 * NT, tok=1)
                    pair(False)
                    A.leave(PAIRS - 1)
                    L.leave(PAIRS - 1)
                pair(True)
                out_blocks(False)
                sum_squares(KT)
                mlp(False)
            pe.wait_ge(stage_free, L.at["s"])
            for t in range(NT):
                for g in range(2):
                    turn([(x[:, 4 * g + k, t * P:(t + 1) * P], P) for k in range(4)], C["turn"] - 1)
            assert C["turn"] == TURNS, C["turn"]

        @block.vector
        def _(dve):
            L = Place(b=0, s=2, m=0, hid=0, acc=0)
            S = Place(n=0)
            C = dict(turn=0, t=0, h=0, rms=0)

            def own(ins):
                ins.then_inc(dve_self, 1)
                S.at["n"] += 1
                dve.wait_ge(dve_self, S.count("n"))

            def mod_reduce():
                raw = mod_raw[L.at["m"] % 2][:, :]
                dve.wait_ge(mod_product, L.count("m", FIRST_MODS - 1))
                for c, prod in enumerate((mod_prod, raw)):
                    ins = dve.tensor_reduce(mod_part[:, c, :], prod.rearrange("p (k n) -> p n k", k=KT), AX_X, ALU.add)
                ins.then_inc(mod_reduced, 1)

            def mod_out(index):
                dve.wait_ge(mod_mm, L.count("m", -1))
                b = 6 + L.at["m"] % 2
                dve.tensor_scalar(mod[:, ds(index, 1), :].rearrange("p a c -> p (a c)"), bank(b, 2),
                                  mod_bias[:, ds(index, 1)], None, ALU.add).then_inc(mod_done, 1)
                L.at["m"] += 1

            def turn_out_(outs):
                b = 6 + C["turn"] % 2
                dve.wait_ge(turn_mm, C["turn"] + 1)
                ins = outs(b * BANK)
                ins.then_inc(turn_out, 1)
                C["turn"] += 1

            def no_squares():
                own(dve.memset(tmp[2][:, 0:N], 0.0))

            def add_square(t):
                if L.i is not None or L.at["acc"] >= 1:
                    dve.wait_ge(acc_done, L.count("acc"))
                dve.wait_ge(sq_done, L.count("acc", -1))
                dve.tensor_tensor(tmp[2][:, 0:N], tmp[2][:, 0:N], tmp[t][:, 0:N], ALU.add).then_inc(acc_done, 1)
                L.at["acc"] += 1

            def inverse_root():
                C["rms"] += 1
                dve.wait_ge(mean_root, C["rms"])
                dve.reciprocal(root[:, :], root[:, :]).then_inc(mean_inverse, 1)
                L.at["s"] += 1
                dve.wait_ge(stage_free, L.at["s"])

            def norm(layer, which, sums=True):
                n = 2 * layer + which
                scale = layer * MODS + (3 * which + 1) * KT
                dve.wait_ge(mod_done, scale + KT)
                g0 = VEC["norm1_g" if which == 0 else "norm2_g"][0] + layer * KT
                gv = vec[:, g0:g0 + KT].unsqueeze(2).to_broadcast([P, KT, 2])
                own(dve.scalar_tensor_tensor(gain[:, n, :, :], mod[:, scale:scale + KT, :], 1.0, gv,
                                             ALU.add, ALU.mult))
                if sums:
                    inverse_root()
                shift = layer * MODS + 3 * which * KT

                def scaled(j):
                    if C["h"]:
                        dve.wait_ge(h_lo_done, C["h"])
                    for a, z, c in SEGS:
                        ins = dve.scalar_tensor_tensor(tmp[j % 2][:, a:z], x[:, j, a:z], gain[:, n, j, c:c + 1],
                                                       rstd[:, a:z], ALU.mult, ALU.mult)
                    ins.then_inc(t_done, 1)
                    C["t"] += 1
                scaled(0)
                for j in range(KT):
                    if j + 1 < KT:
                        scaled(j + 1)
                    C["h"] += 1
                    dve.wait_ge(t_done, C["t"] - (1 if j + 1 < KT else 0))
                    dve.wait_ge(h_hi_done, C["h"])
                    for a, z, c in SEGS:
                        ins = dve.scalar_tensor_tensor(h_lo[:, j, a:z], tmp[j % 2][:, a:z],
                                                       mod[:, shift + j, c:c + 1], h_hi[:, j, a:z].bitcast(F32),
                                                       ALU.add, ALU.subtract)
                    ins.then_inc(h_lo_done, 1)

            def low_rows(dst, src, hi, n):
                for j in range(n):
                    C["h"] += 1
                    dve.wait_ge(h_hi_done, C["h"])
                    dve.tensor_tensor(dst[:, j, :], src[:, j, :], hi[:, j, :].bitcast(F32),
                                      ALU.subtract).then_inc(h_lo_done, 1)

            def residual(j, gate):
                dve.wait_ge(stage_done, L.count("s", 1))
                dve.wait_ge(stage_free, L.count("s"))
                tile = x[:, ds(j, 1), :].rearrange("p a n -> p (a n)")
                for v, xt, c in parts(L.at["s"], tile):
                    ins = dve.scalar_tensor_tensor(xt, v, mod[:, ds(gate, 1), c:c + 1].rearrange("p a c -> p (a c)"), xt,
                                                   ALU.mult, ALU.add)
                ins.then_inc(stage_free, 1)
                L.at["s"] += 1

            def out_blocks(layer, mods):
                no_squares()
                with dve.Fori(0, KT // 2) as i:
                    L.enter(i, s=2, m=2 if mods else 0, acc=2)
                    for k in range(2):
                        if mods:
                            mod_reduce()
                        residual(i * 2 + k, i * 2 + (layer * MODS + 2 * KT + k))
                        if mods:
                            mod_out(i * 2 + (5 * KT + k))
                        add_square(k)
                    L.leave(KT // 2)

            def chunk(gate, m0, squares=False):
                for k in range(2 * HT):
                    mods = m0 is not None and k in MLP_MODS
                    if mods:
                        mod_reduce()
                    if k < HT:
                        dve.wait_ge(stage_done, L.count("s", 1))
                        dve.wait_ge(relu_done, L.count("hid", -1))
                        if k == 0:
                            dve.wait_ge(stage_free, L.count("s"))
                        else:
                            dve.wait_ge(hid_lo_done, L.count("hid"))
                        dve.scalar_tensor_tensor(cols3(tmp[1][:, 0:N]), stage_ps(L.at["s"]), 0.0,
                                                 cols3(tmp[0][:, 0:N]), ALU.max, ALU.mult).then_inc(stage_free, 1)
                        L.at["s"] += 1
                        dve.wait_ge(stage_free, L.count("s"))
                        dve.wait_ge(hid_hi_done, L.count("hid", -1))
                        dve.tensor_tensor(hid_lo[:, k, :], tmp[1][:, 0:N], hid_hi[:, k, :].bitcast(F32),
                                          ALU.subtract).then_inc(hid_lo_done, 1)
                        L.at["hid"] += 1
                    else:
                        for half in range(2):
                            j = (k - HT) * 2 + half
                            residual(j, gate + j)
                            if squares:
                                add_square(half)
                    if mods:
                        mod_out(m0 + MLP_MODS.index(k))

            def mlp(layer, mods):
                gate = layer * MODS + 5 * KT
                dve.wait_ge(h_lo_done, C["h"])
                with dve.Fori(0, CHUNKS - 1) as c:
                    L.enter(c, s=3 * HT, hid=HT, m=6 if mods else 0)
                    chunk(gate, c * 6 + MODS if mods else None)
                    L.leave(CHUNKS - 1)
                if layer < LAYERS - 1:
                    no_squares()
                chunk(gate, (CHUNKS - 1) * 6 + MODS if mods else None, layer < LAYERS - 1)

            turn_out_(lambda b: dve.tensor_copy(mod_bias[:, :], ps[:, b:b + 2 * MODS]))
            turn_out_(lambda b: dve.tensor_copy(vec[:, :], ps[:, b:b + VROWS]))
            dve.wait_ge(cond_act, 1)
            own(dve.tensor_scalar(cond_tmp[:, :, :], cond_tmp[:, :, :], 1.0, None, ALU.add))
            own(dve.reciprocal(cond_tmp[:, :, :], cond_tmp[:, :, :]))
            for k, name in enumerate(("c", "c_ctx")):
                a, z = VEC[name]
                ins = dve.tensor_tensor(cond[:, :, k], cond_tmp[:, :, k], vec[:, a:z], ALU.mult)
            ins.then_inc(cond_ready, 1)
            for m in range(MOD_SLOTS):
                mod_out(m)
            for t in range(NT):
                for g in range(2):
                    turn_out_(lambda b: dve.tensor_copy(x[:, 4 * g:4 * g + 4, t * P:(t + 1) * P],
                                                        ps[:, b:b + 4 * P].rearrange("p (k n) -> p k n", k=4)))
            no_squares()
            for j in range(KT):
                add_square(j % 2)
                if j % 2 == 1:
                    mod_out(MOD_SLOTS + j // 2)
            inverse_root()
            for m in range(MOD_SLOTS + KT // 2, FIRST_MODS):
                mod_out(m)
            norm(0, 0, False)

            pad = tmp[1]
            dve.wait_ge(h_lo_done, C["h"])
            for c in (0, NS + 1, NS + 2, N + 3):
                ins = dve.memset(pad[:, c:c + 1], 0.0)
            own(ins)
            taps, bias0 = VEC["conv_w"][0], VEC["conv_b"][0]
            W2 = N + 2
            with dve.Fori(0, KT // 2) as i:
                L.enter(i, s=6, m=6)
                S.enter(i, n=6)
                for f in range(2):
                    mod_reduce()
                    L.at["s"] += 1
                    mod_out(i * 6 + (FIRST_MODS + 3 * f))
                    mod_reduce()
                    dve.wait_ge(stage_done, L.count("s", 1))
                    dve.wait_ge(stage_free, L.count("s"))
                    dst = [pad[:, 1:1 + 2 * TB].rearrange("p (t n) -> p t n", t=2),
                           pad[:, 1 + 2 * TB:1 + NS], pad[:, NS + 3:N + 3]]
                    for o, (v, g, _) in zip(dst, parts(L.at["s"], tmp[0])):
                        ins = dve.tensor_tensor(o, v, g, ALU.mult)
                    ins.then_inc(stage_free, 1)
                    L.at["s"] += 1
                    mod_out(i * 6 + (FIRST_MODS + 3 * f + 1))
                    mod_reduce()
                    dve.wait_ge(stage_free, L.count("s"))
                    col = [vec[:, ds(i * 2 + (taps + w * KT + f), 1)] for w in range(3)]
                    own(dve.tensor_scalar(tmp[2][:, 0:W2], pad[:, 0:W2], col[0],
                                          vec[:, ds(i * 2 + (bias0 + f), 1)], ALU.mult, ALU.add))
                    for w in (1, 2):
                        own(dve.scalar_tensor_tensor(tmp[2][:, 0:W2], pad[:, w:w + W2], col[w], tmp[2][:, 0:W2],
                                                     ALU.mult, ALU.add))
                    dve.wait_ge(stage_done, L.count("s", 1))
                    out = v32[:, ds(i * 2 + f, 1), :].rearrange("p a n -> p (a n)")
                    cv = [tmp[2][:, 0:2 * TB].rearrange("p (t n) -> p t n", t=2), tmp[2][:, 2 * TB:NS],
                          tmp[2][:, NS + 2:W2]]
                    for c, (v, o, _) in zip(cv, parts(L.at["s"], out)):
                        ins = dve.tensor_tensor(o, v, c, ALU.mult)
                    ins.then_inc(stage_free, 1)
                    L.at["s"] += 1
                    mod_out(i * 6 + (FIRST_MODS + 3 * f + 2))
                S.leave(KT // 2)
                L.leave(KT // 2)
            low_rows(h_lo, v32, h_hi, KT)
            out_blocks(0, True)
            norm(0, 1)
            mlp(0, True)
            if LAYERS > 1:
                norm(1, 0)
                def latent_out(dst):
                    dve.wait_ge(stage_done, L.at["s"] - 1)
                    dve.tensor_copy(cols3(dst), stage_ps(L.at["s"])).then_inc(stage_free, 1)
                    L.at["s"] += 1

                def sum_latent(n):
                    no_squares()
                    for j in range(n):
                        add_square(j % 2)

                def latent_norm(t, n, g0):
                    inverse_root()
                    for j in range(n):
                        dve.scalar_tensor_tensor(t[:, j, 0:N], t[:, j, 0:N], vec[:, g0 + j:g0 + j + 1], rstd[:, :],
                                                 ALU.mult, ALU.mult).then_inc(t_done, 1)
                        C["t"] += 1

                for j in range(QT):
                    latent_out(ql[:, j, :])
                sum_latent(QT)
                latent_out(ckv[:, 0, 0:N])
                latent_norm(ql, QT, VEC["q_norm_g"][0])
                for j in range(1, CT):
                    latent_out(ckv[:, j, 0:N])
                sum_latent(CT)
                turn_out_(lambda b: dve.tensor_copy(ckv[:, :, N:KEYS], ps[:, b:b + CT * P].rearrange(
                    "p (k n) -> p k n", k=CT)))
                latent_out(kpe_t[:, :])
                dve.wait_ge(t_done, C["t"])
                low_rows(ql_lo, ql, ql_hi, QT)
                latent_norm(ckv, CT, VEC["kv_norm_g"][0])
                dve.wait_ge(t_done, C["t"])
                low_rows(ckv_lo, ckv, ckv_hi, CT)
                for a, z in groups(NT, 4):
                    turn_out_(lambda b: dve.tensor_copy(kpe[:, a:z, :], ps[:, b:b + (z - a) * P].rearrange(
                        "p (k n) -> p k n", k=z - a)[:, :, P - ROPE:P]))
                turn_out_(lambda b: dve.tensor_copy(ckv_out[:, :], ps[:, b:b + KVR]))

                dve.wait_ge(gains_in, 16 * 4)
                dve.wait_ge(turn_out, C["turn"])

                def halves(ap):
                    return ap.rearrange("p t (a s d) -> p t a s d", a=2, s=2)

                def gains(g, tiles):
                    return g[:, NOPE:QK].unsqueeze(1).to_broadcast([P, tiles, ROPE])

                dve.tensor_tensor(rot_cos[:, :, :], trig[:, 0, :, :], gains(g_q, NT), ALU.mult)
                for s in range(2):
                    ins = dve.tensor_tensor(halves(rot_sin[:, :, :])[:, :, :, s, :], halves(trig[:, 1, :, :])[:, :, :, s, :],
                                            halves(gains(g_q, NT))[:, :, :, 1 - s, :], ALU.mult)
                dve.tensor_tensor(g_qk[:, :], g_q[:, 0:NOPE], g_k[:, 0:NOPE], ALU.mult)
                own(dve.tensor_tensor(kpe_rot[:, :, :], kpe[:, :, :], gains(g_k, KTILES), ALU.mult))
                dve.tensor_tensor(rot_a[:, :, :], kpe_rot[:, 0:NT, :], trig[:, 0, :, :], ALU.mult)
                for s in range(2):
                    ins = dve.tensor_tensor(halves(rot_b[:, :, :])[:, :, :, s, :],
                                            halves(kpe_rot[:, 0:NT, :])[:, :, :, 1 - s, :],
                                            halves(trig[:, 1, :, :])[:, :, :, s, :], ALU.mult)
                own(ins)
                own(dve.tensor_tensor(kpe_rot[:, 0:NT, :], rot_a[:, :, :], rot_b[:, :, :], ALU.add))
                dve.wait_ge(x_spilled, 16)
                for t in range(KTILES):
                    ins = dve.tensor_tensor_reduce(junk[:, :, :].rearrange("p a n -> p (a n)")[:, t * ROPE:(t + 1) * ROPE],
                                                   kpe[:, t, :], kpe[:, t, :], 1.0 / QK, 0.0, ALU.mult,
                                                   ALU.add, kpe_sq[:, t:t + 1])
                own(ins)
                dve.wait_ge(new_stored, 32)

                A = Place(j=0, u=0, g=0, m=0, r=0)

                def unit_out(ins):
                    ins.then_inc(unit_free, 1)
                    A.at["u"] += 1

                def unit_low(out, in_, hi):
                    A.at["hi"] += 1
                    dve.wait_ge(unit_hi, A.count("hi"))
                    unit_out(dve.tensor_tensor(out, in_, hi.bitcast(F32), ALU.subtract))

                A.at["hi"] = 0

                def v_units(k):
                    for a, z in groups(KTILES, 4):
                        b0 = unit_ps(k)
                        unit_low(v_cols(v_lo, a, z), ps[:, b0:b0 + (z - a) * 2 * VD].rearrange(
                            "p (t h n) -> p t h n", h=2, n=VD), v_cols(v_hi, a, z))
                        k += 1

                def turn_units(k, s):
                    for hi, lo, tiles in ((qT_hi[s], qT_lo[s], NT), (kT_hi[s], kT_lo[s], KTILES)):
                        for a, z in groups(tiles, 4):
                            b0 = unit_ps(k)
                            unit_low(lo[0:QK, a * P:z * P], ps[0:QK, b0:b0 + (z - a) * P], hi[0:QK, a * P:z * P])
                            k += 1

                def qk_units(k, before=None):
                    for i, (a, z) in enumerate(groups(NT, 2)):
                        if before is not None and i in (1, 3):
                            over_sums(i // 2, before)
                        dve.wait_ge(unit_done, A.count("u", -1))
                        b0 = unit_ps(k)
                        unit_out(dve.tensor_copy(q_tok[:, a:z, :, :].rearrange("p t h n -> p (t h n)"),
                                                 ps[:, b0:b0 + (z - a) * 2 * QK]))
                        k += 1
                    if before is not None:
                        over_sums(2, before)
                    for a, z in groups(KTILES, 4):
                        dve.wait_ge(unit_done, A.count("u", -1))
                        b0 = unit_ps(k)
                        unit_out(dve.tensor_copy(k_tok[:, a:z, :, 0:NOPE], ps[:, b0:b0 + (z - a) * 2 * NOPE].rearrange(
                            "p (t h n) -> p t h n", h=2, n=NOPE)))
                        k += 1

                def squares(lo, hi):
                    for i in range(lo, min(hi, 2 * NT + 2 * KTILES)):
                        if i < 2 * NT:
                            row = q_tok[:, i // 2, i % 2, :]
                        else:
                            row = k_tok[:, (i - 2 * NT) // 2, i % 2, 0:NOPE]
                        n = QK if i < 2 * NT else NOPE
                        ins = dve.tensor_tensor_reduce(junk[:, i - lo, 0:n], row, row, 1.0 / QK, 0.0, ALU.mult, ALU.add,
                                                       ssq[:, i:i + 1])
                    own(ins)

                def squares_end():
                    k = ssq[:, 2 * NT:].rearrange("p (t h) -> p t h", h=2)
                    dve.tensor_tensor(k, k, kpe_sq[:, :].unsqueeze(2).to_broadcast([P, KTILES, 2]),
                                      ALU.add).then_inc(ssq_done, 1)

                def rotate_and_scale():
                    for h in range(2):
                        qr = q_tok[:, :, h, NOPE:QK]
                        dve.tensor_tensor(rot_a[:, :, :], qr, rot_cos[:, :, :], ALU.mult)
                        for s in range(2):
                            ins = dve.tensor_tensor(halves(rot_b[:, :, :])[:, :, :, s, :], halves(qr)[:, :, :, 1 - s, :],
                                                    halves(rot_sin[:, :, :])[:, :, :, s, :], ALU.mult)
                        own(ins)
                        own(dve.tensor_tensor(qr, rot_a[:, :, :], rot_b[:, :, :], ALU.add))
                    kn = k_tok[:, :, :, 0:NOPE].rearrange("p t h n -> p (t h) n")
                    own(dve.tensor_tensor(kn, kn, g_qk[:, :].unsqueeze(1).to_broadcast([P, 2 * KTILES, NOPE]), ALU.mult))
                    A.at["r"] += 1
                    dve.wait_ge(r_root, A.count("r"))
                    own(dve.reciprocal(r_tok[:, :], r_tok[:, :]))
                    q = q_tok[:, :, :, :].rearrange("p t h n -> p (t h) n")
                    dve.tensor_tensor(q, q, r_tok[:, 0:2 * NT].unsqueeze(2).to_broadcast([P, 2 * NT, QK]), ALU.mult)
                    rk = r_tok[:, 2 * NT:]
                    dve.tensor_tensor(kn, kn, rk.unsqueeze(2).to_broadcast([P, 2 * KTILES, NOPE]), ALU.mult)
                    rk2 = rk.rearrange("p (t h) -> p t h", h=2)
                    for h in range(2):
                        ins = dve.tensor_tensor(k_tok[:, :, h, NOPE:QK], kpe_rot[:, :, :],
                                                rk2[:, :, h].unsqueeze(2).to_broadcast([P, KTILES, ROPE]), ALU.mult)
                    ins.then_inc(tok_ready, 1)

                def max_out(t):
                    n = NP if t == NT - 1 else NS + P
                    dve.wait_ge(max_mm, A.count("m", -1))
                    dve.tensor_reduce(row_max[:, t:t + 1], ps[:, 0:n], AX_X, ALU.max).then_inc(max_free, 1)
                    A.at["m"] += 1

                def max_rows(k, s):
                    dve.wait_ge(unit_done, A.count("u", -1))
                    b0 = unit_ps(k)
                    unit_out(dve.scalar_tensor_tensor(
                        qT_hi[s][QK:QROWS, :].rearrange("r (t n) -> r t n", n=P),
                        ps[0:NT, b0:b0 + P].unsqueeze(1).to_broadcast([NT, NT, P]), -1.0,
                        ident[0:NT, 0:NT].unsqueeze(2).to_broadcast([NT, NT, P]), ALU.mult, ALU.mult))

                def over_sums(qb, p):
                    cols = slice(qb * BANK, qb * BANK + (NP if qb == 2 else BANK))
                    dve.wait_ge(o_free, A.count("g", -(3 + 4 + qb)))
                    own(dve.reciprocal(sums[:, cols], sums[:, cols]))
                    o = o32[:, ds(p, 1), cols].rearrange("p a n -> p (a n)")
                    dve.tensor_tensor(o, o, sums[:, cols], ALU.mult).then_inc(sums_used, 1)
                    if qb == 2:
                        A.at["g"] += 6

                def pair(first, last, before):
                    v_units(0)
                    turn_units(U_V, 1)
                    if not last:
                        qk_units(U_V + U_TURN, before if not first else None)
                        dve.wait_ge(unit_free, A.count("u"))
                    else:
                        for qb in range(3):
                            over_sums(qb, before)
                    for t in range(NT):
                        max_out(t)
                        if not last and t < NT - 1:
                            squares(5 * t, 5 * t + 5)
                        if not last and t == NT - 2:
                            squares_end()
                    max_rows(U_V + U_TURN + U_QK, 1)
                    if not last:
                        rotate_and_scale()
                        turn_units(U_V + U_TURN + U_QK + U_MAX, 0)
                        for t in range(NT):
                            max_out(t)
                        max_rows(U_V + U_TURN + U_QK + U_MAX + U_TURN, 0)

                for qb in range(3):
                    dve.memset(sums[:, qb * BANK:min((qb + 1) * BANK, N)], 1.0).then_inc(sums_used, 1)
                qk_units(0)
                dve.wait_ge(unit_free, A.count("u"))
                for t in range(NT - 1):
                    squares(5 * t, 5 * t + 5)
                squares_end()
                rotate_and_scale()
                turn_units(U_QK, 0)
                for t in range(NT):
                    max_out(t)
                max_rows(U_QK + U_TURN, 0)
                pair(True, False, None)
                with dve.Fori(1, PAIRS - 1) as p:
                    A.enter(p - 1, u=U_PAIR, g=6, m=2 * NT, r=1, hi=U_V + 2 * U_TURN)
                    S.enter(p - 1, n=NT - 1 + 6 + 3)
                    pair(False, False, p - 1)
                    S.leave(PAIRS - 2)
                    A.leave(PAIRS - 2)
                pair(False, True, PAIRS - 2)
                for qb in range(3):
                    over_sums(qb, PAIRS - 1)
                dve.wait_ge(sums_used, 3 + 3 * PAIRS)
                low_rows(h_lo, o32, h_hi, KT)
                dve.wait_ge(x_back, 16)
                out_blocks(1, False)
                norm(1, 1)
                mlp(1, False)
            dve.wait_ge(stage_free, L.at["s"])
            for t in range(NT):
                for g in range(2):
                    turn_out_(lambda b: dve.tensor_copy(y_out[:, t, 4 * g * P:4 * (g + 1) * P], ps[:, b:b + 4 * P]))


def groups(n, size):
    return [(a, min(a + size, n)) for a in range(0, n, size)]


def v_cols(t, a, z):
    return t[:, a:z, :].rearrange("p t (g n) -> p t g n", g=3)[:, :, 0:3:2, :]


def constants():
    import numpy as np
    grid_w, axis, theta = 64, ROPE // 2, np.float32(10000.0)
    pos = np.arange(NS)
    inv = np.power(theta, -np.arange(0, axis, 2, dtype=np.float32) / np.float32(axis)).astype(np.float32)
    trig = np.zeros((P, 2, NT, ROPE), np.float32)
    trig[:, 0] = 1.0
    for a, where in enumerate((pos // grid_w, pos % grid_w)):
        angle = where.astype(np.float32)[:, None] * inv[None]
        for s in range(2):
            cols = slice(a * axis + s * axis // 2, a * axis + (s + 1) * axis // 2)
            trig[:, 0, :NS // P, cols] = np.cos(angle).reshape(NS // P, P, -1).transpose(1, 0, 2)
            trig[:, 1, :NS // P, cols] = (np.sin(angle) * (2 * s - 1)).reshape(NS // P, P, -1).transpose(1, 0, 2)
    return {"ident": np.eye(P, dtype=np.float32), "trig": trig}


_INS = ["x_prompt", "x_sample", "cache_ckv", "cache_kpe", "c", "c_ctx", "norm1_g", "norm2_g", "mod_w", "mod_b",
        "mlp_w1", "mlp_w2", "sc_w_in", "sc_conv_w", "sc_conv_b", "sc_w_out", "mla_w_dq", "mla_q_norm_g",
        "mla_w_uq", "mla_w_dkv", "mla_kv_norm_g", "mla_w_ukv", "mla_qn_g", "mla_kn_g", "mla_w_o"]
_OUTS = [((1, NP, D), "float32"), ((1, NS, D), "float32"), ((1, 1, NP, KVR), "float32"), ((1, 1, NP, ROPE), "float32")]


def kernel(**inputs):
    import numpy as _np
    import concourse.bacc as _bacc
    from concourse.bass_utils import run_bass_kernel_spmd as _run

    nc = _bacc.Bacc("TRN2", target_bir_lowering=False, num_devices=1)
    arrays, tensors, outs = {}, {}, []
    data = {name: inputs[name] for name in _INS}
    data.update(constants())
    for name, a in data.items():
        a = _np.ascontiguousarray(a)
        arrays[f"in_{name}_dram"] = a
        tensors[name] = nc.dram_tensor(f"in_{name}_dram", a.shape, mybir.dt.from_np(a.dtype), kind="ExternalInput").ap()
    for i, (shape, dtype) in enumerate(_OUTS):
        outs.append(nc.dram_tensor(f"out_{i}_dram", shape, mybir.dt.from_np(_np.dtype(dtype)), kind="ExternalOutput").ap())
    build(nc, tensors, outs)
    r = _run(nc, [arrays], core_ids=[0])
    return tuple(r.results[0][f"out_{i}_dram"] for i in range(len(_OUTS)))
```
